# Optimizing a Trainium2 kernel written in Bass

```python
import math
import jax, jax.numpy as jnp
from jax import lax
import numpy as np

D_MODEL = 2048
BATCH = 1
SEQ = 256
DEPTH = 1

HEAD_DIM = 64
A_HEADS = 16
A_KV_HEADS = 2
WINDOW = 128
BLOCK = 128
B_HEADS = 16
KV_RANK = 256
IDX_HEADS = 16
IDX_DIM = 64
TOPK_MAX = 256
NUM_BUCKETS = 32
MAX_DISTANCE = 128
D_FF = 5632
CONV_WIDTH = 3
EPS = 1e-6
NEG_INF = -1e30
IDX_SCALE = IDX_DIM ** -0.5 * IDX_HEADS ** -0.5
MIX_WIDTH = (A_HEADS + B_HEADS) * HEAD_DIM

A_Q = A_HEADS * HEAD_DIM
A_KV = A_KV_HEADS * HEAD_DIM
B_Q = B_HEADS * HEAD_DIM
I_Q = IDX_HEADS * IDX_DIM
IN_WIDTH = A_Q + 2 * A_KV + B_Q + KV_RANK + I_Q + IDX_DIM + IDX_HEADS
SPLIT_POINTS = (
    A_Q,
    A_Q + A_KV,
    A_Q + 2 * A_KV,
    A_Q + 2 * A_KV + B_Q,
    A_Q + 2 * A_KV + B_Q + KV_RANK,
    A_Q + 2 * A_KV + B_Q + KV_RANK + I_Q,
    A_Q + 2 * A_KV + B_Q + KV_RANK + I_Q + IDX_DIM,
)


def rms_norm(x, g):
    xf = x.astype(jnp.float32)
    y = xf * lax.rsqrt(jnp.mean(xf * xf, axis=-1, keepdims=True) + EPS)
    return (y * g.astype(jnp.float32)).astype(x.dtype)

def rel_bucket(dist):
    n = jnp.maximum(dist, 0)
    max_exact = NUM_BUCKETS // 2
    nf = jnp.maximum(n, 1).astype(jnp.float32)
    large = max_exact + (jnp.log(nf / max_exact) / math.log(MAX_DISTANCE / max_exact)
                         * (NUM_BUCKETS - max_exact)).astype(jnp.int32)
    large = jnp.minimum(large, NUM_BUCKETS - 1)
    return jnp.where(n < max_exact, n, large)

def swa_attention(q, k, v, sinks, rel_table):
    Bsz, T, H, D = q.shape
    nblk = T // BLOCK
    G = H // A_KV_HEADS
    qb = q.reshape(Bsz, nblk, BLOCK, A_KV_HEADS, G, D)
    pad = ((0, 0), (BLOCK, 0), (0, 0), (0, 0))
    kp = jnp.pad(k, pad).reshape(Bsz, nblk + 1, BLOCK, A_KV_HEADS, D)
    vp = jnp.pad(v, pad).reshape(Bsz, nblk + 1, BLOCK, A_KV_HEADS, D)
    kb = jnp.concatenate([kp[:, :-1], kp[:, 1:]], axis=2)
    vb = jnp.concatenate([vp[:, :-1], vp[:, 1:]], axis=2)
    s = jnp.einsum('bnqkgd,bnskd->bnkgqs', qb, kb).astype(jnp.float32) * (D ** -0.5)
    i = jnp.arange(BLOCK, dtype=jnp.int32)[:, None]
    j = jnp.arange(2 * BLOCK, dtype=jnp.int32)[None, :]
    dist = i + BLOCK - j
    in_window = (dist >= 0) & (dist < WINDOW)
    key_pos = jnp.arange(nblk, dtype=jnp.int32)[:, None, None] * BLOCK - BLOCK + j[None]
    valid = in_window[None] & (key_pos >= 0)
    bias = jnp.transpose(rel_table[rel_bucket(dist)], (2, 0, 1))
    bias = bias.reshape(A_KV_HEADS, G, BLOCK, 2 * BLOCK).astype(jnp.float32)
    s = jnp.where(valid[None, :, None, None], s + bias[None, None], NEG_INF)
    sink = sinks.astype(jnp.float32).reshape(A_KV_HEADS, G)[None, None, :, :, None, None]
    m = jnp.maximum(jnp.max(s, axis=-1, keepdims=True), sink)
    e = jnp.exp(s - m)
    p = e / (jnp.sum(e, axis=-1, keepdims=True) + jnp.exp(sink - m))
    o = jnp.einsum('bnkgqs,bnskd->bnqkgd', p.astype(v.dtype), vb)
    return o.reshape(Bsz, T, H * D)

def dsa_attention(q, c_kv, w_uk, w_uv, q_idx, k_idx, w_idx, rel_table):
    Bsz, T, H, D = q.shape
    nblk = T // BLOCK
    topk = min(TOPK_MAX, T // 4)
    scale = D ** -0.5
    key_pos = jnp.arange(T, dtype=jnp.int32)

    def one_block(blk):
        start = blk * BLOCK
        qpos = start + jnp.arange(BLOCK, dtype=jnp.int32)
        qi = lax.dynamic_slice_in_dim(q_idx, start, BLOCK, axis=1)
        wi = lax.dynamic_slice_in_dim(w_idx, start, BLOCK, axis=1)
        qb = lax.dynamic_slice_in_dim(q, start, BLOCK, axis=1)
        dots = jnp.einsum('bqhd,bsd->bqhs', qi, k_idx).astype(jnp.float32)
        index_score = jnp.einsum('bqh,bqhs->bqs', wi.astype(jnp.float32),
                                 jax.nn.relu(dots)) * IDX_SCALE
        causal = key_pos[None, :] <= qpos[:, None]
        index_score = jnp.where(causal[None], index_score, NEG_INF)
        _, sel = lax.top_k(index_score, topk)
        c_sel = jax.vmap(lambda ck, ix: ck[ix])(c_kv, sel)
        q_lat = jnp.einsum('bqhd,hrd->bqhr', qb, w_uk)
        s = jnp.einsum('bqhr,bqkr->bqhk', q_lat, c_sel).astype(jnp.float32) * scale
        dist = qpos[None, :, None] - sel
        bias = jnp.moveaxis(rel_table[rel_bucket(dist)], -1, 2).astype(jnp.float32)
        s = jnp.where((dist >= 0)[:, :, None, :], s + bias, NEG_INF)
        p = jax.nn.softmax(s, axis=-1).astype(c_sel.dtype)
        o_lat = jnp.einsum('bqhk,bqkr->bqhr', p, c_sel)
        o = jnp.einsum('bqhr,hrd->bqhd', o_lat, w_uv)
        return o.reshape(Bsz, BLOCK, H * D)

    out = lax.map(one_block, jnp.arange(nblk, dtype=jnp.int32))
    return jnp.transpose(out, (1, 0, 2, 3)).reshape(Bsz, T, H * D)

def conv_ffn(h, w_up, conv_w, conv_b, w_down):
    u, g = jnp.split(h @ w_up, 2, axis=-1)
    u = lax.conv_general_dilated(
        u, conv_w[:, None, :], window_strides=(1,), padding=((CONV_WIDTH - 1, 0),),
        dimension_numbers=('NWC', 'WIO', 'NWC'), feature_group_count=D_FF) + conv_b
    return (jax.nn.silu(u) * g) @ w_down

def first_inputs(seed: int = 0) -> dict:
    key = jax.random.key(seed)
    ks = jax.random.split(key, 20)
    f32 = jnp.float32
    nrm = lambda k, shape, s: jax.random.normal(k, shape, f32) * s
    return {
        "x": nrm(ks[0], (BATCH, SEQ, D_MODEL), 1.0),
        "c": nrm(ks[1], (BATCH, D_MODEL), 1.0),
        "w_mod": nrm(ks[2], (DEPTH, D_MODEL, 6 * D_MODEL), D_MODEL ** -0.5),
        "b_mod": nrm(ks[3], (DEPTH, 6 * D_MODEL), 0.02),
        "norm_attn": 1.0 + nrm(ks[4], (DEPTH, D_MODEL), 0.02),
        "w_in": nrm(ks[5], (DEPTH, D_MODEL, IN_WIDTH), D_MODEL ** -0.5),
        "attn_sinks": nrm(ks[6], (DEPTH, A_HEADS), 0.5),
        "kv_norm": 1.0 + nrm(ks[7], (DEPTH, KV_RANK), 0.02),
        "w_uk": nrm(ks[8], (DEPTH, B_HEADS, KV_RANK, HEAD_DIM), KV_RANK ** -0.5),
        "w_uv": nrm(ks[9], (DEPTH, B_HEADS, KV_RANK, HEAD_DIM), KV_RANK ** -0.5),
        "rel_bias": nrm(ks[10], (NUM_BUCKETS, A_HEADS + B_HEADS), 0.3),
        "w_out": nrm(ks[11], (DEPTH, MIX_WIDTH, D_MODEL), MIX_WIDTH ** -0.5),
        "norm_ffn": 1.0 + nrm(ks[12], (DEPTH, D_MODEL), 0.02),
        "w_up": nrm(ks[13], (DEPTH, D_MODEL, 2 * D_FF), D_MODEL ** -0.5),
        "conv_w": nrm(ks[14], (DEPTH, CONV_WIDTH, D_FF), CONV_WIDTH ** -0.5),
        "conv_b": nrm(ks[15], (DEPTH, D_FF), 0.02),
        "w_down": nrm(ks[16], (DEPTH, D_FF, D_MODEL), D_FF ** -0.5),
        "norm_final": 1.0 + nrm(ks[17], (D_MODEL,), 0.02),
    }

def first_block(x, c, w_mod, b_mod, norm_attn, w_in, attn_sinks, kv_norm, w_uk, w_uv,
              rel_bias, w_out, norm_ffn, w_up, conv_w, conv_b, w_down, norm_final):
    Bsz, T, _ = x.shape
    rel_a = rel_bias[:, :A_HEADS]
    rel_b = rel_bias[:, A_HEADS:]
    c_act = jax.nn.silu(c)
    for l in range(DEPTH):
        mod = c_act @ w_mod[l] + b_mod[l]
        sh1, sc1, g1, sh2, sc2, g2 = [m[:, None, :] for m in jnp.split(mod, 6, axis=-1)]

        h = rms_norm(x, norm_attn[l]) * (1.0 + sc1) + sh1
        qa, ka, va, qb, ckv, qi, ki, wi = jnp.split(h @ w_in[l], SPLIT_POINTS, axis=-1)
        qa = qa.reshape(Bsz, T, A_HEADS, HEAD_DIM)
        ka = ka.reshape(Bsz, T, A_KV_HEADS, HEAD_DIM)
        va = va.reshape(Bsz, T, A_KV_HEADS, HEAD_DIM)
        qb = qb.reshape(Bsz, T, B_HEADS, HEAD_DIM)
        ckv = rms_norm(ckv, kv_norm[l])
        qi = qi.reshape(Bsz, T, IDX_HEADS, IDX_DIM)
        out_a = swa_attention(qa, ka, va, attn_sinks[l], rel_a)
        out_b = dsa_attention(qb, ckv, w_uk[l], w_uv[l], qi, ki, wi, rel_b)
        mix = jnp.concatenate([out_a, out_b], axis=-1) @ w_out[l]
        x = x + g1 * mix

        h = rms_norm(x, norm_ffn[l]) * (1.0 + sc2) + sh2
        x = x + g2 * conv_ffn(h, w_up[l], conv_w[l], conv_b[l], w_down[l])
    return rms_norm(x, norm_final)


DEPTH_2 = 2

N_A_LAYERS = DEPTH_2 // 2
N_B_LAYERS = DEPTH_2 - N_A_LAYERS
GM_WIDTH = 2 * D_MODEL
GM_GROUPS = 16
GM_GROUP_DIM = GM_WIDTH // GM_GROUPS
CHUNK = 128
N_HEADS = 16
QK_NOPE_DIM = 128
QK_ROPE_DIM = 64
V_HEAD_DIM = 128
Q_LORA_RANK = 512
KV_LORA_RANK = 512
ATTN_WIDTH = N_HEADS * V_HEAD_DIM
ROPE_THETA = 10000.0
Q_BLOCK = 128


def rms_norm_2(x, g):
    xf = x.astype(jnp.float32)
    y = xf * lax.rsqrt(jnp.mean(xf * xf, axis=-1, keepdims=True) + EPS)
    return (y * g.astype(jnp.float32)).astype(x.dtype)

def layer_norm(x, g, b):
    xf = x.astype(jnp.float32)
    mu = jnp.mean(xf, axis=-1, keepdims=True)
    xc = xf - mu
    y = xc * lax.rsqrt(jnp.mean(xc * xc, axis=-1, keepdims=True) + EPS)
    return (y * g.astype(jnp.float32) + b.astype(jnp.float32)).astype(x.dtype)

def ada_mod(c, w, b):
    return (jax.nn.silu(c) @ w + b)[:, None, :]

def rope_tables(seq_len):
    pos = jnp.arange(seq_len, dtype=jnp.float32)
    inv_freq = ROPE_THETA ** (-jnp.arange(0, QK_ROPE_DIM, 2, dtype=jnp.float32) / QK_ROPE_DIM)
    ang = pos[:, None] * inv_freq[None, :]
    return jnp.cos(ang), jnp.sin(ang)

def apply_rope(x, cos, sin):
    xf = x.astype(jnp.float32)
    x1, x2 = jnp.split(xf, 2, axis=-1)
    return jnp.concatenate([x1 * cos - x2 * sin, x2 * cos + x1 * sin], axis=-1).astype(x.dtype)

def gmlp_mixer(h, w_in, ln_g, ln_b, w_s, b_s, w_out):
    B, S, _ = h.shape
    u, v, z = jnp.split(h @ w_in, 3, axis=-1)
    u = jax.nn.gelu(u)
    v = layer_norm(jax.nn.gelu(v), ln_g, ln_b)
    causal = jnp.tril(jnp.ones((CHUNK, CHUNK), dtype=bool))
    ws = jnp.where(causal, w_s, 0.0).astype(v.dtype)
    vc = v.reshape(B, S // CHUNK, CHUNK, GM_GROUPS, GM_GROUP_DIM)
    mixed = jnp.einsum('gts,bnsgc->bntgc', ws, vc) + b_s.T[None, None, :, :, None].astype(v.dtype)
    y = u * mixed.reshape(B, S, GM_WIDTH) * jax.nn.silu(z)
    return y @ w_out

def mla_shared_kv(h, w_dkv, g_kva, w_ukv, g_kn, g_kr, cos, sin):
    B, S, _ = h.shape
    c_kv, k_r = jnp.split(h @ w_dkv, [KV_LORA_RANK], axis=-1)
    c_kv = rms_norm_2(c_kv, g_kva)
    kv = (c_kv @ w_ukv).reshape(B, S, N_HEADS, QK_NOPE_DIM + V_HEAD_DIM)
    k_nope, v = jnp.split(kv, [QK_NOPE_DIM], axis=-1)
    k_nope = rms_norm_2(k_nope, g_kn)
    k_rope = apply_rope(rms_norm_2(k_r, g_kr), cos, sin)
    return k_nope, k_rope, v

def causal_block_attention(q_nope, q_rope, k_nope, k_rope, v):
    B, S, H, _ = q_nope.shape
    nb = S // Q_BLOCK
    scale = (QK_NOPE_DIM + QK_ROPE_DIM) ** -0.5
    qn = q_nope.reshape(B, nb, Q_BLOCK, H, QK_NOPE_DIM).transpose(1, 0, 2, 3, 4)
    qr = q_rope.reshape(B, nb, Q_BLOCK, H, QK_ROPE_DIM).transpose(1, 0, 2, 3, 4)
    k_pos = jnp.arange(S)

    def block(args):
        qn_b, qr_b, i = args
        s = (jnp.einsum('bqhd,bkhd->bhqk', qn_b, k_nope)
             + jnp.einsum('bqhr,bkr->bhqk', qr_b, k_rope)).astype(jnp.float32) * scale
        q_pos = i * Q_BLOCK + jnp.arange(Q_BLOCK)
        s = jnp.where(k_pos[None, :] <= q_pos[:, None], s, -jnp.inf)
        p = jax.nn.softmax(s, axis=-1).astype(v.dtype)
        return jnp.einsum('bhqk,bkhd->bqhd', p, v)

    o = lax.map(block, (qn, qr, jnp.arange(nb)))
    return o.transpose(1, 0, 2, 3, 4).reshape(B, S, H, V_HEAD_DIM)

def mla_mixer(h, k_nope, k_rope, v, w_in, g_qa, w_uq, g_qn, g_qr, w_out, cos, sin):
    B, S, _ = h.shape
    c_q, z = jnp.split(h @ w_in, [Q_LORA_RANK], axis=-1)
    q = (rms_norm_2(c_q, g_qa) @ w_uq).reshape(B, S, N_HEADS, QK_NOPE_DIM + QK_ROPE_DIM)
    q_nope, q_rope = jnp.split(q, [QK_NOPE_DIM], axis=-1)
    q_nope = rms_norm_2(q_nope, g_qn)
    q_rope = apply_rope(rms_norm_2(q_rope, g_qr), cos[:, None, :], sin[:, None, :])
    o = causal_block_attention(q_nope, q_rope, k_nope, k_rope, v)
    y = o.reshape(B, S, ATTN_WIDTH) * jax.nn.silu(z)
    return y @ w_out

def second_inputs(seed: int = 0) -> dict:
    key = jax.random.key(seed)
    ks = iter(jax.random.split(key, 32))
    D = D_MODEL

    def nrm(shape, std):
        return std * jax.random.normal(next(ks), shape, jnp.float32)

    return {
        "x": nrm((BATCH, SEQ, D), 1.0),
        "c": nrm((BATCH, D), 1.0),
        "ada_w": nrm((DEPTH_2, D, 3 * D), 0.5 * D ** -0.5),
        "ada_b": nrm((DEPTH_2, 3 * D), 0.02),
        "norm_g": 1.0 + nrm((DEPTH_2, D), 0.02),
        "a_w_in": nrm((N_A_LAYERS, D, 3 * GM_WIDTH), D ** -0.5),
        "a_ln_g": 1.0 + nrm((N_A_LAYERS, GM_WIDTH), 0.02),
        "a_ln_b": nrm((N_A_LAYERS, GM_WIDTH), 0.02),
        "a_w_s": nrm((N_A_LAYERS, GM_GROUPS, CHUNK, CHUNK), CHUNK ** -0.5),
        "a_b_s": 1.0 + nrm((N_A_LAYERS, GM_GROUPS, CHUNK), 0.1),
        "a_w_out": nrm((N_A_LAYERS, GM_WIDTH, D), GM_WIDTH ** -0.5),
        "kv_ada_w": nrm((D, 2 * D), 0.5 * D ** -0.5),
        "kv_ada_b": nrm((2 * D,), 0.02),
        "kv_norm_g": 1.0 + nrm((D,), 0.02),
        "kv_w_dkv": nrm((D, KV_LORA_RANK + QK_ROPE_DIM), D ** -0.5),
        "kv_g_kva": 1.0 + nrm((KV_LORA_RANK,), 0.02),
        "kv_w_ukv": nrm((KV_LORA_RANK, N_HEADS * (QK_NOPE_DIM + V_HEAD_DIM)), KV_LORA_RANK ** -0.5),
        "kv_g_kn": 1.0 + nrm((QK_NOPE_DIM,), 0.02),
        "kv_g_kr": 1.0 + nrm((QK_ROPE_DIM,), 0.02),
        "b_w_in": nrm((N_B_LAYERS, D, Q_LORA_RANK + ATTN_WIDTH), D ** -0.5),
        "b_g_qa": 1.0 + nrm((N_B_LAYERS, Q_LORA_RANK), 0.02),
        "b_w_uq": nrm((N_B_LAYERS, Q_LORA_RANK, N_HEADS * (QK_NOPE_DIM + QK_ROPE_DIM)), Q_LORA_RANK ** -0.5),
        "b_g_qn": 1.0 + nrm((N_B_LAYERS, QK_NOPE_DIM), 0.02),
        "b_g_qr": 1.0 + nrm((N_B_LAYERS, QK_ROPE_DIM), 0.02),
        "b_w_out": nrm((N_B_LAYERS, ATTN_WIDTH, D), ATTN_WIDTH ** -0.5),
    }

def second_block(x, c, ada_w, ada_b, norm_g, a_w_in, a_ln_g, a_ln_b, a_w_s, a_b_s, a_w_out,
              kv_ada_w, kv_ada_b, kv_norm_g, kv_w_dkv, kv_g_kva, kv_w_ukv, kv_g_kn, kv_g_kr,
              b_w_in, b_g_qa, b_w_uq, b_g_qn, b_g_qr, b_w_out):
    cos, sin = rope_tables(x.shape[1])
    k_nope = k_rope = v = None
    for i in range(DEPTH_2):
        if i == N_A_LAYERS:
            kv_shift, kv_scale = jnp.split(ada_mod(c, kv_ada_w, kv_ada_b), 2, axis=-1)
            h_kv = rms_norm_2(x, kv_norm_g) * (1.0 + kv_scale) + kv_shift
            k_nope, k_rope, v = mla_shared_kv(h_kv, kv_w_dkv, kv_g_kva, kv_w_ukv, kv_g_kn, kv_g_kr, cos, sin)
        shift, scale, gate = jnp.split(ada_mod(c, ada_w[i], ada_b[i]), 3, axis=-1)
        h = rms_norm_2(x, norm_g[i]) * (1.0 + scale) + shift
        if i < N_A_LAYERS:
            out = gmlp_mixer(h, a_w_in[i], a_ln_g[i], a_ln_b[i], a_w_s[i], a_b_s[i], a_w_out[i])
        else:
            j = i - N_A_LAYERS
            out = mla_mixer(h, k_nope, k_rope, v, b_w_in[j], b_g_qa[j], b_w_uq[j], b_g_qn[j],
                            b_g_qr[j], b_w_out[j], cos, sin)
        x = x + gate * out
    return x


def setup_inputs(seed=0):
    out = dict(first_inputs(seed))
    for name, value in second_inputs(seed + 1).items():
        if name != "x":
            out[name + "_2"] = value
    return out


def reference(
    x, c, w_mod, b_mod, norm_attn, w_in, attn_sinks, kv_norm, w_uk, w_uv, rel_bias, w_out,
    norm_ffn, w_up, conv_w, conv_b, w_down, norm_final, c_2, ada_w_2, ada_b_2, norm_g_2,
    a_w_in_2, a_ln_g_2, a_ln_b_2, a_w_s_2, a_b_s_2, a_w_out_2, kv_ada_w_2, kv_ada_b_2,
    kv_norm_g_2, kv_w_dkv_2, kv_g_kva_2, kv_w_ukv_2, kv_g_kn_2, kv_g_kr_2, b_w_in_2, b_g_qa_2,
    b_w_uq_2, b_g_qn_2, b_g_qr_2, b_w_out_2,
):
    x = first_block(
        x, c, w_mod, b_mod, norm_attn, w_in, attn_sinks, kv_norm, w_uk, w_uv, rel_bias, w_out,
        norm_ffn, w_up, conv_w, conv_b, w_down, norm_final,
    )
    return second_block(
        x, c_2, ada_w_2, ada_b_2, norm_g_2, a_w_in_2, a_ln_g_2, a_ln_b_2, a_w_s_2, a_b_s_2,
        a_w_out_2, kv_ada_w_2, kv_ada_b_2, kv_norm_g_2, kv_w_dkv_2, kv_g_kva_2, kv_w_ukv_2,
        kv_g_kn_2, kv_g_kr_2, b_w_in_2, b_g_qa_2, b_w_uq_2, b_g_qn_2, b_g_qr_2, b_w_out_2,
    )


_drawn_inputs = setup_inputs


def setup_inputs(seed=0):
    import zlib

    import numpy as np

    out = dict(_drawn_inputs(seed))
    spreads = {}
    factors = {'norm_attn': 4.13,
     'attn_sinks': 8.0,
     'kv_norm': 8.0,
     'norm_ffn': 4.026,
     'conv_b': 6.727,
     'norm_final': 2.774,
     'ada_b_2': 3.715,
     'norm_g_2': 8.0,
     'a_ln_g_2': 8.0,
     'a_ln_b_2': 8.0,
     'a_b_s_2': 3.934,
     'kv_ada_b_2': 8.0,
     'kv_norm_g_2': 21.92,
     'kv_g_kva_2': 24.38,
     'kv_g_kn_2': 26.513,
     'kv_g_kr_2': 31.123,
     'b_g_qa_2': 8.0,
     'b_g_qn_2': 26.022,
     'b_g_qr_2': 33.134}
    for name, (base, spread) in spreads.items():
        noise = np.random.default_rng([zlib.crc32(name.encode()), seed]).standard_normal(out[name].shape)
        drawn = base * np.exp(spread * noise) if base else spread * noise
        out[name] = __import__('jax').numpy.asarray(drawn.astype(out[name].dtype))
    for name, factor in factors.items():
        out[name] = (out[name] * factor).astype(out[name].dtype)
    return out
```

```python
from contextlib import ExitStack

import numpy as np
import concourse.bass as bass
from concourse import mybir

F32 = mybir.dt.float32
F32R = mybir.dt.float32r
ALU = mybir.AluOpType
ACT = mybir.ActivationFunctionType
AX = mybir.AxisListType.X

P = 128
T = 256
D = 2048
KT = D // P
EPS = 1e-6
NEG = -1e30
TAKEN = -3e38
TOPK = 64
D_FF = 5632
FF_STEPS = D_FF // 512
GM = 4096
GM_STEPS = GM // 512
HALF_PARTS = 28
HALVES = 4
SLOTS = 4

U_OUT, U_FF, U_V = 32, 48, 180
U_GM = U_V + 32
U_MLA = U_GM + 8 + (GM_STEPS - 1) * 12 + 4
J_OUT, J_FF = 12, 16
J_V = J_FF + 2 + (FF_STEPS - 1) * 6 + 4
J_GM = J_V + 8
J_MLA = J_GM + 2 + (GM_STEPS - 1) * 6 + 4
UNITS = U_MLA + 58

COLS = {}
_n = 0
for _name, _w in (("b_mod", 8 * HALF_PARTS), ("norm_attn", 16), ("norm_ffn", 16), ("norm_final", 16),
                  ("norm_a", 16), ("norm_kv", 16), ("norm_b", 16), ("conv", 16 * FF_STEPS),
                  ("kv_norm", 2), ("g_kva", 4), ("g_qa", 4), ("g_kn", 1), ("g_qn", 1),
                  ("g_kr", 1), ("g_krs", 1), ("g_qr", 1), ("g_qrs", 1), ("c", 32)):
    COLS[_name] = _n
    _n += _w
NCOLS = _n
CST = {}
_n = 0
for _name, _w in (("ident", 128), ("causal3", 384), ("triu", 128), ("cos", 256), ("sin", 256), ("blk", 128)):
    CST[_name] = _n
    _n += _w
NCST = _n


class Where:

    def __init__(self):
        self.i, self.per = None, {}

    def __call__(self, kind, n):
        return n if self.i is None else self.i * self.per[kind] + n


def build(nc, stream, mods, xT, cols, cst, relb, onehot, sinks, rowpar, wsT, out):
    with ExitStack() as ctx:
        sems = {}

        def S(name):
            if name not in sems:
                sems[name] = ctx.enter_context(nc.semaphore(name))
            return sems[name]

        BASE = 16512
        K = 1024
        place = {"at": BASE}

        def sb(name, shape, dt=F32, at=None):
            n = 4 * int(np.prod(shape[1:]))
            if at is None:
                at = place["at"]
                place["at"] = at + (n + 31) // 32 * 32
            return nc.alloc_sbuf_tensor_at(name, shape, dt, offset=at)

        raw = sb("raw", [P, SLOTS, 2048])
        hi = sb("hi", [P, HALVES, 1024], F32R)
        lo = sb("lo", [P, HALVES, 1024], F32R)
        AT_MOD = place["at"]
        mraw = sb("mraw", [P, 2, 2, 1024])
        macc = sb("macc", [P, 2, 1024])
        x = sb("x", [P, KT, T])
        AT_H = place["at"]
        h_hi = sb("h_hi", [P, KT, T], F32R)
        h_lo = sb("h_lo", [P, KT, T], F32R)
        col = sb("col", [P, NCOLS])
        con = sb("con", [P, NCST])
        ones = sb("ones", [P, P])
        cact = sb("cact", [P, 32])
        ctab = sb("ctab", [P, 10, 16])
        cuse = sb("cuse", [P, 16])
        modc = sb("modc", [P, 8 * HALF_PARTS])
        coef = sb("coef", [P, 16])
        rs = sb("rs", [P, T])
        rinv = sb("rinv", [P, T])
        small = sb("small", [P, 64])
        AT = place["at"]
        END = 229344

        def area(items):
            at, made = AT, []
            for name, shape, dt in items:
                made.append(sb(name, shape, dt, at=at))
                at += 4 * int(np.prod(shape[1:]))
            assert at <= END, (items[0][0], at - END)
            return made

        KB = 1024
        wa, wb, wc, wd = area([(n, [P, 4, T], F32) for n in ("wa", "wb", "wc", "wd")])
        g6, csq, c_hi, c_lo, qa, qb, qi, vb, vtok, wtok, bring, sring, pt, isc, sel, tiny = area([
            ("g6", [P, 4, T], F32), ("csq", [P, 2, T], F32), ("c_hi", [P, 2, T], F32R), ("c_lo", [P, 2, T], F32R),
            ("qa", [P, 8, T], F32), ("qb", [P, 8, T], F32), ("qi", [P, 8, T], F32), ("vb", [P, 2, 1024], F32),
            ("vtok", [P, 2, P], F32), ("wtok", [P, 2, 16], F32), ("bring", [P, 3, 384], F32),
            ("sring", [P, 4, 384], F32), ("pt", [P, 2, 384], F32), ("isc", [P, 384], F32),
            ("sel", [P, 384], F32), ("tiny", [P, 96], F32)])
        relu = sb("relu", [P, 4, 512], at=AT + 18 * KB)
        kb = sb("kb", [P, 8, T], at=AT + 26 * KB)
        at = AT + (42 + 1 + 4) * KB + 512
        va = sb("va", [P, T], at=at)
        wiT = sb("wiT", [16, T], at=at + KB)
        bvec = sb("bvec", [16, 2, 384], at=at + 2 * KB)
        rel33 = sb("rel33", [33, 32], at=at + 6 * KB)
        hot33 = sb("hot33", [33, 768], at=at + 6 * KB + 128)
        facc = sb("facc", [P, KT, T], at=AT + 16 * KB)
        ubuf = sb("ubuf", [P, 4, T + 2], at=AT + 32 * KB)
        cwi = sb("cwi", [P, 16], at=AT + 37 * KB)
        y_hi = sb("y_hi", [P, 4, T], F32R, at=AT + 53 * KB)
        y_lo = sb("y_lo", [P, 4, T], F32R, at=AT_MOD + 20 * KB)
        lnrow = sb("lnrow", [P, 2, 512], at=AT + 12 * KB)
        v = sb("v", [P, 2, GM], at=AT + 16 * KB)
        vs = sb("vs", [P, 2, 512], at=AT + 48 * KB)
        wst = sb("wst", [P, 2, P], at=AT + 52 * KB)
        bsrow = sb("bsrow", [P, 2, P], at=AT + 57 * KB)
        stats = sb("stats", [P, 2, 8, 6], at=AT + 58 * KB)
        mv = sb("mv", [P, 2, 2], at=AT + 58 * KB + 512)
        rstd = sb("rstd", [P, 2], at=AT + 58 * KB + 544)
        kn = sb("kn", [P, 16, T], at=AT + 16 * KB)
        vm = sb("vm", [P, 2, 2048], at=AT + 32 * KB)
        kr = sb("kr", [P, T], at=AT + 48 * KB)
        qr = sb("qr", [P, 8, T], at=AT + 49 * KB)
        tiny2 = sb("tiny2", [P, 96], at=AT + 57 * KB)
        sring2 = sb("sring2", [P, 4, 384], at=AT)
        pt2 = sb("pt2", [P, 2, 384], at=AT + 6 * KB)
        zs = sb("zs", [P, 16, T], at=AT_MOD)
        m_hi = sb("m_hi", [P, 4, T], F32R, at=AT_MOD + 16 * KB)
        m_lo = sb("m_lo", [P, 4, T], F32R, at=AT_MOD + 20 * KB)
        qn = sb("qn", [P, 16, T], at=AT_H)

        ps = ctx.enter_context(nc.psum_tensor("ps", [P, 8, 512], F32))
        scratch = nc.dram_tensor("bias_rows", (2, 16, P, 384), F32)

        def pair(J):
            p = J % 3
            return ps[:, 2 * p:2 * p + 2, :].rearrange("p b (m t) -> p (b m) t", m=2)

        def pair2(J):
            p = J % 3
            return ps[:, 2 * p:2 * p + 2, :]

        def c0(name, k=0, n=1):
            return col[:, COLS[name] + k:COLS[name] + k + n]

        def k0_(name, n):
            return con[:, CST[name]:CST[name] + n]

        raw_full = [S(f"raw_full{i}") for i in range(SLOTS)]
        mod_full = [S(f"mod_full{i}") for i in range(2)]
        evac = [S(f"evac{i}") for i in range(3)]
        hi_ready = S("hi_ready")
        lo_ready = S("lo_ready")
        half_used = S("half_used")
        consts = S("consts")
        NCONST = 6
        mod_sum = S("mod_sum")
        colsum = S("colsum")
        modc_ready = S("modc_ready")
        x_ok = S("x_ok")
        sq_ready, stat_sum = S("sq_ready"), S("stat_sum")
        root_ready, rinv_ready = S("root_ready"), S("rinv_ready")
        coef_ready, ht_ready = S("coef_ready"), S("ht_ready")
        h_hi_ready, h_lo_ready = S("h_hi_ready"), S("h_lo_ready")

        block = ctx.enter_context(nc.Block())

        SPAN = {}
        at_h = 0
        for J, n in enumerate([8, 4] + [8] * 6 + [1] * 4 + [8] * 4 + [8, 8]):
            SPAN[J] = (at_h, n)
            at_h += n
        for g in range(8):
            SPAN[J_V + g] = (2 * U_V + 8 * g, 8)
        SPAN[J_GM], SPAN[J_GM + 1] = (2 * U_GM, 8), (2 * U_GM + 8, 8)
        for c in range(4):
            SPAN[J_V - 4 + c] = (2 * U_V - 8 + 2 * c, 2)
            SPAN[J_MLA - 4 + c] = (2 * U_MLA - 8 + 2 * c, 2)
        at_h = 2 * U_MLA
        for J, n in enumerate([8, 4] + [2] * 8 + [8] * 5 + [2] * 8 + [8] * 4):
            SPAN[J_MLA + J] = (at_h, n)
            at_h += n
        assert at_h == 2 * UNITS

        def last_half(J):
            return SPAN[J][0] + SPAN[J][1]

        HEADS = 16
        att_scores, att_sc, att_max, att_negm = S("att_scores"), S("att_sc"), S("att_max"), S("att_negm")
        att_exp, att_den, att_rden, att_prob = S("att_exp"), S("att_den"), S("att_rden"), S("att_prob")
        att_turned, att_pt, att_pv = S("att_turned"), S("att_pt"), S("att_pv")
        att_o, att_ohi, att_olo = S("att_o"), S("att_ohi"), S("att_olo")
        bias_full = [S(f"bias_full{i}") for i in range(3)]
        bias_sum = S("bias_sum")

        def order(a, k):
            return (k // 2 + 8 * (k % 2)) if a == 0 else k

        def idx_ops(it):
            return 2 * (it + 1) if it < 8 else 16 + 4 * (it - 7)

        def idx_heads(it):
            return range(4 * (it // 2) + it % 2, 4 * (it // 2) + 4, 2) if it < 8 else \
                range(8 * (it // 2 - 4) + it % 2, 8 * (it // 2 - 4) + 8, 2)

        ZERO = 0

        def exp_count(n):
            return 3 * min(n, 16) + 2 * max(0, n - 16)

        def unit_steps(first, last, lag, sched, do):
            for u in range(first, last):
                do(u)
                for f in sched.get(u, ()):
                    f()

        @block.sync
        def _(sp):
            def load(u, i=None, per=0):
                at = u if i is None else i * per + u
                if u >= SLOTS:
                    sp.wait_ge(lo_ready, 2 * (at - SLOTS) + 2)
                sp.dma_start(raw[:, u % SLOTS, :], stream[at]).then_inc(raw_full[u % SLOTS], 16)

            def load_mod(m, i=None, per=0):
                at = m if i is None else i * per + m
                if m >= 2:
                    sp.wait_ge(mod_sum, 2 * (at - 1))
                sp.dma_start(mraw[:, m % 2, :, :].rearrange("p k n -> p (k n)"), mods[at])\
                    .then_inc(mod_full[m % 2], 16)

            sp.dma_start(col[:], cols).then_inc(consts, 16)
            load_mod(0)
            load_mod(1)
            sp.dma_start(tiny[:, 0:16], sinks.partition_broadcast(P)).then_inc(consts, 16)
            sp.dma_start(con[:], cst).then_inc(consts, 16)
            sp.dma_start(rel33[0:32, :], relb).then_inc(consts, 16)
            sp.dma_start(hot33[:], onehot).then_inc(consts, 16)
            sp.dma_start(x[:], xT).then_inc(consts, 16)
            for u in range(4):
                load(u)
            for u in range(2):
                load(4 + u)
            with sp.Fori(0, 16) as i:
                for m in range(2):
                    load_mod(2 + m, i, 2)
            sp.wait_ge(S("bias_rows_ready"), 1)
            for a in range(2):
                sp.dma_start(scratch.ap()[a], bvec[:, a:a + 1, :].to_broadcast([16, P, 384])).then_inc(S("bias_rows"), 16)
            for m in range(34, 36):
                load_mod(m)
            with sp.Fori(0, 7) as i:
                for k in range(4):
                    load(6 + k, i, 4)
                    load_mod(36 + k, i, 4)
            for k in range(2):
                load(34 + k)
                load_mod(64 + k)
            sp.wait_ge(S("bias_rows"), 32)
            for n in range(2 * HEADS):
                a, h = n // HEADS, order(n // HEADS, n % HEADS)
                if n >= 3:
                    sp.wait_ge(att_sc, n - 2)
                for j, (c, w) in enumerate(((0, 256), (128, 128))):
                    sp.dma_start(bring[:, n % 3, 256 * j:256 * j + w],
                                 bass.AP(scratch, (a * 16 + h) * P * 384 + 127 + c, [[383, P], [1, w]]))\
                        .then_inc(bias_full[n % 3], 16)
            for k in range(14):
                load(36 + k)
                load_mod(66 + k)
            for k in range(2):
                load(50 + k)
            for k in range(8):
                load(52 + k)
            with sp.Fori(0, FF_STEPS - 1) as i:
                load_mod(80, i, 8)
                load_mod(81, i, 8)
                for k in range(12):
                    load(60 + k, i, 12)
                    if k < 6:
                        load_mod(82 + k, i, 8)
            for k in range(4):
                load(U_V + k)
            with sp.Fori(0, 4) as i:
                for k in range(8):
                    if k % 4 == 0:
                        load_mod(160 + k // 4, i, 2)
                    load(U_V + 4 + k, i, 8)
            for k in range(8):
                load(U_GM + 4 + k)

            def load_rows(s):
                sp.dma_start(lnrow[:].rearrange("p a n -> p (a n)"), rowpar[s, 0:1024].partition_broadcast(P))\
                    .then_inc(S("lnrow"), 16)
                sp.dma_start(bsrow[:].rearrange("p a n -> p (a n)"), rowpar[s, 1024:1280].partition_broadcast(P))\
                    .then_inc(S("bsrow"), 16)
                sp.dma_start(wst[:].rearrange("p a n -> p (a n)"), wsT[s]).then_inc(S("wst"), 16)

            sp.wait_ge(h_lo_ready, 16 * 3)
            sp.wait_ge(h_hi_ready, 16 * 3)
            load_rows(0)
            with sp.Fori(0, GM_STEPS - 1) as i:
                load_mod(168, i, 8)
                load_mod(169, i, 8)
                for k in range(12):
                    load(U_GM + 12 + k, i, 12)
                    if k < 6:
                        load_mod(170 + k, i, 8)
                    if k == 8:
                        sp.wait_ge(S("mixed"), 2 * (i + 1))
                        sp.wait_ge(S("wmix"), i + 1)
                        load_rows(i + 1)
            for k in range(UNITS - U_MLA):
                load(U_MLA + k)
            sp.wait_ge(x_ok, 5)
            sp.dma_start(out, x[:]).then_inc(S("stored"), 16)
            sp.wait_ge(S("stored"), 16)

        @block.scalar
        def _(act):
            act.wait_ge(consts, 16 * NCONST)

            def split(u, i=None):
                at = u if i is None else i * 12 + u
                act.wait_ge(raw_full[u % SLOTS], 16 * (u // SLOTS + 1) if i is None else i * 48 + 16 * (u // SLOTS + 1))
                for h in range(2):
                    if 2 * u + h >= HALVES:
                        act.wait_ge(half_used, 2 * at + h - HALVES + 1)
                    act.activation(hi[:, (2 * u + h) % HALVES, :], raw[:, u % SLOTS, 1024 * h:1024 * h + 1024],
                                   ACT.Copy).then_inc(hi_ready, 1)

            def splits(a, b):
                for u in range(a, b):
                    split(u)

            def job_done(J):
                act.wait_ge(half_used, last_half(J))

            def squares(s):
                if s:
                    act.wait_ge(x_ok, [0, 1, 2, 3, 4][s])
                for c in range(4):
                    n = 4 * s + c
                    if n >= 2:
                        act.wait_ge(stat_sum, n - 1)
                    act.activation((wa, wb)[n % 2][:], x[:, 4 * c:4 * c + 4, :], ACT.Square).then_inc(sq_ready, 1)
                act.wait_ge(stat_sum, 4 * s + 4)
                if s:
                    act.wait_ge(rinv_ready, s)
                    act.wait_ge(S("c_rinv"), 1)
                act.activation(rs[:], ps[:, 7, 0:T], ACT.Sqrt, scale=1.0 / D, bias=EPS).then_inc(root_ready, 1)

            def h_rounded(n, shift):
                for k in range(KT):
                    act.wait_ge(ht_ready, 16 * n + 4 * (k // 4) + 4)
                    act.activation(h_hi[:, k, :], (wc, wd)[(k // 4) % 2][:, k % 4, :], ACT.Identity,
                                   bias=modc[:, shift + k:shift + k + 1]).then_inc(h_hi_ready, 1)

            act.activation(cact[:], c0("c", 0, 32), ACT.Silu).then_inc(S("cact"), 1)
            act.wait_ge(S("bias_mm"), 2)
            act.activation(bvec[:, 0, :], ps[0:16, 6, 0:384], ACT.Copy)
            act.activation(bvec[:, 1, :], ps[0:16, 7, 0:384], ACT.Copy).then_inc(S("bias_rows_ready"), 1)
            splits(0, 2)
            squares(0)
            h_rounded(0, 0)
            splits(2, 6)
            job_done(0)
            act.activation(g6[:], pair(0), ACT.Copy).then_inc(evac[0], 1)
            act.wait_ge(evac[0], 1)
            act.activation(csq[:], g6[:, 2:4, :], ACT.Square).then_inc(S("c_sq"), 1)
            splits(6, 8)
            job_done(1)
            act.wait_ge(S("bias_rows"), 32)
            act.activation(va[:], pair(1)[:, 0, :], ACT.Copy)
            act.activation(wiT[:], pair(1)[0:16, 1, :], ACT.Copy, scale=64 ** -0.5 * 16 ** -0.5).then_inc(evac[1], 1)
            splits(8, 12)
            job_done(2)
            act.activation(qi[:, 0:4, :], pair(2), ACT.Copy).then_inc(evac[2], 1)
            act.wait_ge(S("c_sum"), 1)
            act.wait_ge(rinv_ready, 1)
            act.activation(rs[:], ps[:, 7, 0:T], ACT.Sqrt, scale=1.0 / 256, bias=EPS).then_inc(S("c_root"), 1)
            act.wait_ge(S("turned"), 1)
            act.activation(vtok[:], ps[:, 6, 0:256].rearrange("p (a c) -> p a c", a=2), ACT.Copy)
            act.activation(wtok[:], ps[:, 6, 256:288].rearrange("p (a c) -> p a c", a=2), ACT.Copy).then_inc(S("turned_out"), 1)
            for k in range(2):
                act.wait_ge(S("c_norm"), k + 1)
                act.activation(c_hi[:, k, :], g6[:, 2 + k, :], ACT.Copy).then_inc(S("c_hi"), 1)
            splits(12, 16)
            job_done(3)
            act.activation(qi[:, 4:8, :], pair(3), ACT.Copy).then_inc(evac[0], 1)
            for it in range(12):
                act.wait_ge(S("idx_mm"), it + 1)
                if it >= 4:
                    act.wait_ge(S("idx_sum"), idx_ops(it - 4))
                act.activation(relu[:, it % 4, :], ps[:, it % 4, :], ACT.Relu).then_inc(S("idx_relu"), 1)
            splits(16, 20)
            job_done(4)
            act.activation(qa[:, 0:4, :], pair(4), ACT.Copy).then_inc(evac[1], 1)
            splits(20, 24)
            job_done(5)
            act.activation(qa[:, 4:8, :], pair(5), ACT.Copy).then_inc(evac[2], 1)
            splits(24, 28)
            job_done(6)
            act.wait_ge(S("idx_sum"), 32)
            act.activation(qb[:, 0:4, :], pair(6), ACT.Copy).then_inc(evac[0], 1)
            splits(28, 32)
            job_done(7)
            act.activation(qb[:, 4:8, :], pair(7), ACT.Copy).then_inc(evac[1], 1)
            for j in range(2):
                job_done(8 + j)
                act.activation(kb[:, 4 * j:4 * j + 4, :], pair(8 + j), ACT.Copy).then_inc(evac[(8 + j) % 3], 1)
            for j in range(2):
                job_done(10 + j)
                act.activation(vb[:, :, 512 * j:512 * j + 512], pair2(10 + j), ACT.Copy).then_inc(evac[(10 + j) % 3], 1)

            def attention(a):
                sr, tn, pb = (sring, tiny, pt) if a < 2 else (sring2, tiny2, pt2)
                for k in range(HEADS + 4):
                    n = 16 * a + k
                    if k < HEADS:
                        act.wait_ge(att_negm, n + 1)
                        if n >= 4:
                            act.wait_ge(att_prob, 2 * (n - 3))
                        for b, (c, w) in enumerate(((0, 256), (256, 128))):
                            act.activation(sr[:, n % 4, c:c + w], sr[:, n % 4, c:c + w], ACT.Exp,
                                           bias=tn[:, 24 + 2 * (n % 4) + b:25 + 2 * (n % 4) + b],
                                           accum_out=tn[:, 32 + 2 * (n % 4) + b:33 + 2 * (n % 4) + b])\
                                .then_inc(att_exp, 1)
                        if a == 0:
                            h = order(a, k)
                            act.activation(tn[:, 40 + 2 * (n % 4):42 + 2 * (n % 4)],
                                           tn[:, 24 + 2 * (n % 4):26 + 2 * (n % 4)], ACT.Exp,
                                           bias=tn[:, h:h + 1]).then_inc(att_exp, 1)
                    if 3 <= k < HEADS + 3:
                        m = n - 3
                        act.wait_ge(att_turned, m + 1)
                        if m >= 2:
                            act.wait_ge(att_pv, m - 1)
                        act.activation(pb[:, m % 2, :], ps[:, 3 + m % 2, 0:384], ACT.Copy).then_inc(att_pt, 1)
                    if k >= 4 and a < 2 and k % 2 == 1:
                        j = (k - 5) // 2
                        act.wait_ge(att_pv, 16 * a + 2 * j + 2)
                        act.activation(h_hi[:, 8 * a + j, :], ps[:, 5 + 2 * (j % 2), 0:T], ACT.Copy).then_inc(att_ohi, 1)
                    if k >= 4 and a == 2:
                        j = k - 4
                        act.wait_ge(att_o, j + 1)
                        act.activation(h_hi[:, j, :], zs[:, j, :], ACT.Copy).then_inc(att_ohi, 1)

            attention(0)
            attention(1)
            splits(32, 50)
            squares(1)
            h_rounded(1, 48)

            def channels_out(pos, s, J):
                act.wait_ge(half_used, pos)
                act.wait_ge(S("conv"), 12 * s)
                act.activation(ubuf[:, :, 2:2 + T], pair(J), ACT.Copy).then_inc(evac[J % 3], 1)

            def conv_silu(s, first_step=False):
                for m in range(4):
                    act.wait_ge(S("conv"), 12 * s + 9 + m)
                    if m == 0 and first_step is False:
                        act.wait_ge(S("y"), s)
                    act.activation(wb[:, m, :], wa[:, m, :], ACT.Silu, bias=cwi[:, 12 + m:13 + m]).then_inc(S("silu"), 1)

            def y_rounded(s, used, J):
                act.wait_ge(S("y"), s + 1)
                act.wait_ge(half_used, used)
                act.activation(y_hi[:], wc[:], ACT.Copy).then_inc(evac[J % 3], 1)

            splits(50, 54)
            act.wait_ge(S("zeroed"), 1)
            act.wait_ge(half_used, last_half(J_FF))
            act.activation(ubuf[:, :, 2:2 + T], pair(J_FF), ACT.Copy).then_inc(evac[J_FF % 3], 1)
            conv_silu(0, first_step=True)
            splits(54, 56)
            with act.Fori(0, FF_STEPS - 1) as i:
                for k in range(12):
                    split(56 + k, i)
                    if k == 1:
                        y_rounded(i, i * 24 + 2 * 56, J_FF + 1)
                    if k == 5:
                        channels_out(i * 24 + 2 * 60, i + 1, J_FF + 2)
                    if k == 6:
                        conv_silu(i + 1)
            y_rounded(FF_STEPS - 1, 2 * (U_V - 4), J_FF + 1)
            splits(U_V - 4, U_V)
            splits(U_V, U_V + 2)
            squares(2)
            squares(3)
            h_rounded(2, 96)

            def v_out(pos, g, J):
                act.wait_ge(half_used, pos)
                for t in range(2):
                    ins = act.activation(v[:, t, bass.ds(g * 512, 512)], pair2(J)[:, t, :], ACT.Gelu_apprx_tanh)
                ins.then_inc(evac[J % 3], 1)

            splits(U_V + 2, U_V + 6)
            for g in range(8):
                job_done(J_V + g)
                for t in range(2):
                    ins = act.activation(v[:, t, 512 * g:512 * g + 512], pair2(J_V + g)[:, t, :], ACT.Gelu_apprx_tanh)
                ins.then_inc(evac[(J_V + g) % 3], 1)
                if g == 7:
                    act.wait_ge(S("v_var"), 1)
                    act.activation(rstd[:], mv[:, :, 1], ACT.Sqrt, bias=EPS).then_inc(S("v_root"), 1)
                    splits(U_V + 34, U_V + 38)
                else:
                    splits(U_V + 6 + 4 * g, U_V + 10 + 4 * g)

            def gelu_out(J, s):
                act.activation(wa[:], pair(J), ACT.Gelu_apprx_tanh).then_inc(evac[J % 3], 1)

            def tanh_out(J):
                act.activation(wb[:], pair(J), ACT.Tanh, scale=0.5).then_inc(S("tanh"), 1)

            job_done(J_GM)
            gelu_out(J_GM, 0)
            splits(U_V + 38, U_GM + 8)
            with act.Fori(0, GM_STEPS - 1) as i:
                for k in range(12):
                    split(U_GM + 8 + k, i)
                    if k == 1:
                        act.wait_ge(half_used, i * 24 + 2 * (U_GM + 8))
                        act.wait_ge(S("y"), FF_STEPS + i)
                        tanh_out(J_GM + 1)
                        act.wait_ge(S("y"), FF_STEPS + i + 1)
                        act.activation(y_hi[:], wc[:], ACT.Copy).then_inc(evac[(J_GM + 1) % 3], 1)
                    if k == 5:
                        act.wait_ge(half_used, i * 24 + 2 * (U_GM + 12))
                        gelu_out(J_GM + 2, i + 1)
            act.wait_ge(half_used, 2 * (U_MLA - 4))
            tanh_out(J_GM + 1)
            act.wait_ge(S("y"), FF_STEPS + GM_STEPS)
            act.activation(y_hi[:], wc[:], ACT.Copy).then_inc(evac[(J_GM + 1) % 3], 1)
            splits(U_MLA - 4, U_MLA + 2)

            def root(e, wide, scale):
                act.wait_ge(S("n_sum"), e + 1)
                if e >= 2:
                    act.wait_ge(S("n_used"), e - 1)
                if e == 2:
                    act.wait_ge(h_lo_ready, 80)
                act.activation((wc, wd)[e % 2][:].rearrange("p a t -> p (a t)")[:, 0:wide],
                               ps[:, 6:8, :].rearrange("p b t -> p (b t)")[:, 0:wide], ACT.Sqrt,
                               scale=scale, bias=EPS).then_inc(S("n_root"), 1)

            def square(e, src, n):
                if e >= 2:
                    act.wait_ge(S("n_sum"), e - 1)
                act.activation((wa, wb)[e % 2][:, 0:n, :], src, ACT.Square).then_inc(S("n_sq"), 1)

            def c_rounded(j):
                for k in range(4):
                    act.wait_ge(S("n_c"), 4 * j + k + 1)
                    act.activation(m_hi[:, k, :], (kn, qr)[j][:, k, :], ACT.Copy).then_inc(S("m_hi"), 1)

            U, J = U_MLA, J_MLA
            squares(4)
            h_rounded(3, 144)
            splits(U + 2, U + 6)
            job_done(J)
            act.activation(kn[:, 0:4, :], pair(J), ACT.Copy).then_inc(evac[J % 3], 1)
            act.wait_ge(evac[J % 3], J // 3 + 1)
            square(0, kn[:, 0:4, :], 4)
            splits(U + 6, U + 8)
            job_done(J + 1)
            square(1, pair(J + 1)[:, 0:1, :], 1)
            root(0, T, 1 / 512)
            root(1, T, 1 / 64)
            c_rounded(0)
            h_rounded(4, 176)
            for k in range(4):
                splits(U + 8 + k, U + 9 + k)
                job_done(J + 2 + k)
                square(2 + k, pair(J + 2 + k), 4)
                root(2 + k, 1024, 1 / 128)
            for k in range(4):
                splits(U + 12 + k, U + 13 + k)
                job_done(J + 6 + k)
                act.activation(vm[:, :, 512 * k:512 * k + 512], pair2(J + 6 + k), ACT.Copy).then_inc(evac[(J + 6 + k) % 3], 1)
            splits(U + 16, U + 20)
            job_done(J + 10)
            act.activation(qr[:, 0:4, :], pair(J + 10), ACT.Copy).then_inc(evac[(J + 10) % 3], 1)
            act.wait_ge(evac[(J + 10) % 3], (J + 10) // 3 + 1)
            square(6, qr[:, 0:4, :], 4)
            splits(U + 20, U + 24)
            root(6, T, 1 / 512)
            c_rounded(1)
            for k in range(4):
                job_done(J + 11 + k)
                act.activation(zs[:, 4 * k:4 * k + 4, :], pair(J + 11 + k), ACT.Silu).then_inc(evac[(J + 11 + k) % 3], 1)
                splits(U + 24 + 4 * k, U + 28 + 4 * k) if k < 3 else splits(U + 36, U + 37)
            for k in range(4):
                job_done(J + 15 + k)
                square(7 + k, pair(J + 15 + k), 4)
                root(7 + k, 1024, 1 / 128)
                splits(U + 37 + k, U + 38 + k)
            for k in range(2):
                job_done(J + 19 + k)
                square(11 + k, pair(J + 19 + k), 4)
                root(11 + k, 1024, 1 / 64)
                splits(U + 41 + k, U + 42 + k)
            attention(2)
            splits(U + 43, UNITS)

        @block.tensor
        def _(pe):
            pe.wait_ge(consts, 16 * NCONST)
            pe.wait_ge(S("ones"), 2)

            def three(o, w_hi, w_lo, a_hi, a_lo, start, stop, weights_stay):
                for n, (w, a) in enumerate(((w_hi, a_hi), (w_hi, a_lo), (w_lo, a_hi))):
                    lhsT, rhs = (w, a) if weights_stay else (a, w)
                    ins = pe.matmul(o, lhsT, rhs, start=start and n == 0, stop=stop and n == 2, skip_group_check=True)
                return ins

            def job(J, a_hi, a_lo, k0=0, wide=512, turned=False, tiles=None, first=None, i=None, per=24,
                    banks=0, n_halves=None, ready=None):
                h0, n = (first, n_halves) if first is not None else SPAN[J]
                count = J // 3 if i is None else i * 2 + J // 3
                if J >= 3:
                    pe.wait_ge(evac[J % 3], count)
                nk = 1024 // wide
                for q in range(n):
                    h = h0 + q
                    if ready:
                        ready(q)
                    pe.wait_ge(lo_ready, h + 1 if i is None else i * per + h + 1)
                    w_h = hi[:, h % HALVES, :].rearrange("p (k c) -> p k c", k=nk)
                    w_l = lo[:, h % HALVES, :].rearrange("p (k c) -> p k c", k=nk)
                    todo = [(m, k) for m in range(2 if turned else (tiles or wide // P)) for k in range(nk)]
                    for m, k in todo:
                        kt = k0 + q * nk + k
                        begin = q == 0 and k == 0
                        end = q == n - 1 and k == nk - 1
                        if turned:
                            ins = three(pair2(J)[:, m, :], w_h[:, k, :], w_l[:, k, :],
                                        a_hi[:, kt, m * P:m * P + P], a_lo[:, kt, m * P:m * P + P], begin, end, False)
                        else:
                            ins = three(pair(J)[:, m, :], w_h[:, k, m * P:m * P + P], w_l[:, k, m * P:m * P + P],
                                        a_hi[:, kt, :], a_lo[:, kt, :], begin and m % 2 == 0, end, True)
                    ins.then_inc(half_used, 1)

            def column_sums(hp, i=None, two=True):
                at = hp if i is None else i + hp
                pe.wait_ge(mod_sum, 16 * (at + 1))
                if hp >= 1:
                    pe.wait_ge(modc_ready, at)
                for c in range(8):
                    ins = pe.matmul(ps[:, 6, c:c + 1], macc[:, hp % 2 if two else 0, P * c:P * c + P], ones[:, 0:1],
                                    start=True, stop=True)
                ins.then_inc(colsum, 1)

            def norm_sums(s):
                if s:
                    pe.wait_ge(root_ready, s)
                for c in range(4):
                    pe.wait_ge(sq_ready, 4 * s + c + 1)
                    for k in range(4):
                        ins = pe.matmul(ps[:, 7, 0:T], ones[:], (wa, wb)[c % 2][:, k, :],
                                        start=c == 0 and k == 0, stop=c == 3 and k == 3)
                    ins.then_inc(stat_sum, 1)

            def h_there(n):
                def ready(q):
                    pe.wait_ge(h_lo_ready, 16 * n + 2 * q + 2)
                return ready

            def h_all(n):
                pe.wait_ge(h_lo_ready, 16 * n + 16)

            for a in range(2):
                pe.matmul(ps[0:16, 6 + a, 0:384], rel33[:, 16 * a:16 * a + 16], hot33[:, 384 * a:384 * a + 384],
                          start=True, stop=True).then_inc(S("bias_mm"), 1)
            pe.wait_ge(S("bias_rows_ready"), 1)
            for hp in range(4):
                column_sums(hp)
            norm_sums(0)
            job(0, h_hi, h_lo, ready=h_there(0))
            job(1, h_hi, h_lo, wide=256)
            job(2, h_hi, h_lo)
            pe.wait_ge(S("c_sq"), 1)
            pe.wait_ge(root_ready, 1)
            for k in range(2):
                ins = pe.matmul(ps[:, 7, 0:T], ones[:], csq[:, k, :], start=k == 0, stop=k == 1)
            ins.then_inc(S("c_sum"), 1)
            pe.wait_ge(evac[1], 1)
            pe.wait_ge(modc_ready, 4)
            for t in range(2):
                pe.transpose(ps[:, 6, P * t:P * t + P], va[:, P * t:P * t + P], k0_("ident", P))
            for t in range(2):
                ins = pe.transpose(ps[:, 6, 256 + 16 * t:272 + 16 * t], wiT[:, P * t:P * t + P], k0_("ident", P)[0:16, 0:16])
            ins.then_inc(S("turned"), 1)
            job(3, h_hi, h_lo)
            for b in range(3):
                pe.wait_ge(evac[b], (2, 1, 1)[b])
            for it in range(12):
                if it >= 4:
                    pe.wait_ge(S("idx_relu"), it - 3)
                for s, h in enumerate(idx_heads(it)):
                    p0 = 64 * (h % 2)
                    if it < 8:
                        o, q, n = ps[:, it % 4, T * s:T * s + T], qi[p0:p0 + 64, h // 2, P:T], T
                    else:
                        o, q, n = ps[:, it % 4, P * s:P * s + P], qi[p0:p0 + 64, h // 2, 0:P], P
                    ins = pe.matmul(o, q, g6[p0:p0 + 64, 1, 0:n], start=True, stop=True)
                ins.then_inc(S("idx_mm"), 1)
            pe.wait_ge(S("turned_out"), 1)
            column_sums(4)
            pe.wait_ge(S("idx_relu"), 12)
            job(4, h_hi, h_lo)
            job(5, h_hi, h_lo)
            column_sums(5)
            job(6, h_hi, h_lo)
            job(7, h_hi, h_lo)
            column_sums(6)
            pe.wait_ge(S("c_lo"), 2)
            job(8, c_hi, c_lo)
            job(9, c_hi, c_lo)
            job(10, c_hi, c_lo, turned=True)
            job(11, c_hi, c_lo, turned=True)
            for b in range(3):
                pe.wait_ge(evac[b], 4)

            def attention(a):
                sr, pb = (sring, pt) if a < 2 else (sring2, pt2)
                for k in range(HEADS + 4):
                    n = 16 * a + k
                    if k < HEADS:
                        if n >= 3:
                            pe.wait_ge(att_sc, n - 2)
                        h = order(a, k)
                        for q0, c, w in ((P, 0, T), (0, T, P)):
                            o = ps[:, n % 3, c:c + w]
                            if a == 2:
                                p0 = 64 * (h % 2)
                                pe.matmul(o, qn[:, h, q0:q0 + P], kn[:, h, 0:w], start=True, stop=False)
                                ins = pe.matmul(o, qr[p0:p0 + 64, h // 2, q0:q0 + P], kr[p0:p0 + 64, 0:w],
                                                start=False, stop=True)
                            else:
                                p0 = 64 * (k % 2)
                                q = (qa, qb)[a][p0:p0 + 64, k // 2, q0:q0 + P]
                                key = g6[p0:p0 + 64, 0, 0:w] if a == 0 else kb[p0:p0 + 64, k // 2, 0:w]
                                ins = pe.matmul(o, q, key, start=True, stop=True)
                        ins.then_inc(att_scores, 1)
                    if 3 <= k < HEADS + 3:
                        m = n - 3
                        pe.wait_ge(att_prob, 2 * (m + 1))
                        if m >= 2:
                            pe.wait_ge(att_pt, m - 1)
                        for c in range(3):
                            ins = pe.transpose(ps[:, 3 + m % 2, P * c:P * c + P], sr[:, m % 4, P * c:P * c + P], k0_("ident", P))
                        ins.then_inc(att_turned, 1)
                    if k >= 4:
                        m = n - 4
                        j = k - 4
                        pe.wait_ge(att_pt, m + 1)
                        if a < 2:
                            b, p0, w = 5 + 2 * (j // 2 % 2), 64 * (j % 2), 64
                            if 16 * a + j >= 4 and j % 2 == 0:
                                pe.wait_ge(att_olo, (16 * a + j) // 2 - 1)
                            val = (lambda t: vtok[:, t, p0:p0 + 64]) if a == 0 else (lambda t: vb[:, t, 64 * j:64 * j + 64])
                        else:
                            b, p0, w = 5 + 2 * (j % 2), 0, P
                            pe.wait_ge(att_olo, 16)
                            if j >= 2:
                                pe.wait_ge(att_o, j - 1)
                            val = lambda t: vm[:, t, P * j:P * j + P]
                        o = ps[p0:p0 + w, b, :]
                        pe.matmul(o[:, P:T], val(0), pb[:, m % 2, 0:P], start=True, stop=False, skip_group_check=True)
                        pe.matmul(o[:, P:T], val(1), pb[:, m % 2, P:T], start=False, stop=False, skip_group_check=True)
                        pe.matmul(o[:, 0:P], val(0), pb[:, m % 2, T:T + P], start=False, stop=True,
                                  skip_group_check=True).then_inc(att_pv, 1)

            attention(0)
            attention(1)
            pe.wait_ge(att_olo, 16)
            job(12, h_hi, h_lo)
            column_sums(7)
            job(13, h_hi, h_lo)
            job(14, h_hi, h_lo)
            column_sums(8)
            job(15, h_hi, h_lo)
            column_sums(9)
            norm_sums(1)
            job(J_FF, h_hi, h_lo, ready=h_there(1))
            job(J_FF + 1, h_hi, h_lo)
            with pe.Fori(0, FF_STEPS - 1) as i:
                job(J_FF + 2, h_hi, h_lo, first=112, n_halves=8, i=i)
                pe.wait_ge(S("y_lo"), i + 1)
                for c in range(4):
                    job(J_FF + 3 + c, y_hi, y_lo, first=120 + 2 * c, n_halves=2, i=i)
                column_sums(10, i, two=False)
                job(J_FF + 7, h_hi, h_lo, first=128, n_halves=8, i=i)
            pe.wait_ge(S("y_lo"), FF_STEPS)
            for c in range(4):
                job(J_V - 4 + c, y_hi, y_lo)
            norm_sums(2)
            norm_sums(3)
            for g in range(8):
                job(J_V + g, h_hi, h_lo, turned=True, ready=h_there(2) if g == 0 else None)
            job(J_GM, h_hi, h_lo)
            column_sums(20, two=False)
            job(J_GM + 1, h_hi, h_lo)

            def mix(s, i=None):
                pe.wait_ge(S("vs"), s * 2 + 2)
                pe.wait_ge(S("wst_masked"), s + 1)
                pe.wait_ge(modc_ready, s + 21)
                if s is not ZERO:
                    pe.wait_ge(S("mixed"), s * 2)
                for c in range(4):
                    for t in range(2):
                        ins = pe.matmul(ps[:, 6 + c // 2, T * (c % 2) + P * t:T * (c % 2) + P * t + P],
                                        vs[:, t, P * c:P * c + P], wst[:, c // 2, :], start=True, stop=True)
                ins.then_inc(S("wmix"), 1)

            with pe.Fori(0, GM_STEPS - 1) as i:
                mix(i)
                job(J_GM + 2, h_hi, h_lo, first=2 * (U_GM + 8), n_halves=8, i=i)
                pe.wait_ge(S("y_lo"), i + FF_STEPS + 1)
                for c in range(4):
                    job(J_GM + 3 + c, y_hi, y_lo, first=2 * (U_GM + 12 + c), n_halves=2, i=i)
                pe.wait_ge(S("mixed"), i * 2 + 2)
                column_sums(21, i, two=False)
                job(J_GM + 7, h_hi, h_lo, first=2 * (U_GM + 16), n_halves=8, i=i)
            mix(GM_STEPS - 1)
            pe.wait_ge(S("y_lo"), FF_STEPS + GM_STEPS)
            for c in range(4):
                job(J_MLA - 4 + c, y_hi, y_lo)
            pe.wait_ge(S("mixed"), 2 * GM_STEPS)
            norm_sums(4)
            J = J_MLA

            def sums(e, pieces):
                pe.wait_ge(S("n_sq"), e + 1)
                if e:
                    pe.wait_ge(S("n_root"), e)
                side = (wa, wb)[e % 2]
                for o, w, t, start, stop in pieces:
                    ins = pe.matmul(o, w, side[:, t, :] if isinstance(t, int) else side[:, t[0]:t[1], :],
                                    start=start, stop=stop)
                ins.then_inc(S("n_sum"), 1)

            four = [(ps[:, 6, 0:T], ones[:], k, k == 0, k == 3) for k in range(4)]

            def wide(w):
                return [(ps[:, 6 + b, :], w, (2 * b, 2 * b + 2), True, True) for b in range(2)]

            job(J, h_hi, h_lo, ready=h_there(3))
            pe.wait_ge(evac[(J + 1) % 3], (J + 1) // 3)
            for q in range(4):
                h = SPAN[J + 1][0] + q
                pe.wait_ge(lo_ready, h + 1)
                for k in range(8):
                    ins = three(pair(J + 1)[:, q // 2, :], hi[:, h % HALVES, P * k:P * k + P], lo[:, h % HALVES, P * k:P * k + P],
                                h_hi[:, 8 * (q % 2) + k, :], h_lo[:, 8 * (q % 2) + k, :], q == 0 and k == 0, k == 7 and q % 2 == 1, True)
                ins.then_inc(half_used, 1)
            sums(0, four)
            sums(1, [(ps[:, 6, 0:T], k0_("blk", P), 0, True, True)])
            pe.wait_ge(S("m_lo"), 4)
            job(J + 2, m_hi, m_lo)
            for k in range(4):
                job(J + 3 + k, m_hi, m_lo, turned=k == 3)
                sums(2 + k, wide(ones[:]))
            for k in range(3):
                job(J + 7 + k, m_hi, m_lo, turned=True)
            h_all(4)
            job(J + 10, h_hi, h_lo)
            job(J + 11, h_hi, h_lo)
            sums(6, four)
            for k in range(3):
                job(J + 12 + k, h_hi, h_lo)
            pe.wait_ge(S("m_lo"), 8)
            job(J + 15, m_hi, m_lo)
            for k in range(4):
                job(J + 16 + k, m_hi, m_lo)
                sums(7 + k, wide(ones[:]))
            job(J + 20, m_hi, m_lo)
            sums(11, wide(k0_("blk", P)))
            job(J + 21, m_hi, m_lo)
            sums(12, wide(k0_("blk", P)))
            job(J + 22, m_hi, m_lo)
            for b in range(3):
                pe.wait_ge(evac[b], (J + 23 + 2 - b) // 3 if False else len([j for j in range(J + 23) if j % 3 == b]))
            pe.wait_ge(S("qr_done"), 2)
            attention(2)
            pe.wait_ge(att_olo, 32)
            for k in range(4):
                job(J + 23 + k, h_hi, h_lo)

        @block.vector
        def _(dve):
            dve.memset(ones[:], 1.0).then_inc(S("ones"), 1)
            dve.memset(rel33[32:33, :], 1.0).then_inc(S("ones"), 1)
            dve.wait_ge(consts, 16 * NCONST)
            TT, STT, TS = dve.tensor_tensor, dve.scalar_tensor_tensor, dve.tensor_scalar
            MUL, ADD, SUB = ALU.mult, ALU.add, ALU.subtract

            def split(u, i=None):
                for h in range(2):
                    dve.wait_ge(hi_ready, 2 * u + h + 1 if i is None else i * 24 + 2 * u + h + 1)
                    s = (2 * u + h) % HALVES
                    TT(lo[:, s, :], raw[:, u % SLOTS, 1024 * h:1024 * h + 1024], hi[:, s, :].bitcast(F32), SUB)\
                        .then_inc(lo_ready, 1)

            def splits(a, b):
                for u in range(a, b):
                    split(u)

            def job_done(J):
                dve.wait_ge(half_used, last_half(J))

            def mod_unit(m, i=None, per=8, c=None, two=True):
                at = m if i is None else i * per + m
                hp = m // 8
                acc = macc[:, hp % 2 if two else 0, :]
                for j in range(2):
                    kt = 2 * (m % 8) + j
                    if j == 0:
                        dve.wait_ge(mod_full[m % 2], 16 * (m // 2 + 1) if i is None else i * (per * 8) + 16 * (m // 2 + 1))
                    scalar = (c if c is not None else cact)[:, kt:kt + 1] if c is not None or hp < 12 else cact[:, 16 + kt:17 + kt]
                    if kt == 0:
                        free = hp - 1 if two else hp
                        if i is not None:
                            free = i + hp if per == 8 else hp
                        if i is not None or free > 0:
                            dve.wait_ge(colsum, free)
                        TS(acc, mraw[:, m % 2, j, :], scalar, None, MUL).then_inc(mod_sum, 1)
                    else:
                        dve.wait_ge(mod_sum, 2 * at + j)
                        STT(out=acc, in0=mraw[:, m % 2, j, :], scalar=scalar, in1=acc, op0=MUL, op1=ADD)\
                            .then_inc(mod_sum, 1)

            def mod_out(hp, i=None):
                at = hp if i is None else i + hp
                dve.wait_ge(colsum, at + 1)
                TT(modc[:, bass.ds(at * 8, 8)] if i is not None else modc[:, 8 * hp:8 * hp + 8], ps[:, 6, 0:8],
                   col[:, bass.ds(at * 8 + COLS["b_mod"], 8)] if i is not None else c0("b_mod", 8 * hp, 8), ADD)\
                    .then_inc(modc_ready, 1)

            def rinverse(s):
                dve.wait_ge(root_ready, s + 1)
                dve.wait_ge(ht_ready, [0, 16, 32, 32, 48][s]) if s else None
                if s == 1:
                    dve.wait_ge(S("c_norm"), 2)
                if s == 3:
                    dve.wait_ge(x_ok, 3)
                dve.reciprocal(rinv[:], rs[:]).then_inc(rinv_ready, 1)
                dve.wait_ge(rinv_ready, s + 1)

            def make_h(n, scale, norm):
                if n:
                    dve.wait_ge(ht_ready, 16 * n)
                STT(out=coef[:], in0=modc[:, scale:scale + KT], scalar=1.0, in1=c0(norm, 0, KT), op0=ADD, op1=MUL)\
                    .then_inc(coef_ready, 1)
                dve.wait_ge(coef_ready, n + 1)
                shift = scale - KT

                def rest(c):
                    for k in range(4 * c, 4 * c + 4):
                        dve.wait_ge(h_hi_ready, 16 * n + k + 1)
                        STT(out=h_lo[:, k, :], in0=(wc, wd)[c % 2][:, k % 4, :], scalar=modc[:, shift + k:shift + k + 1],
                            in1=h_hi[:, k, :].bitcast(F32), op0=ADD, op1=SUB).then_inc(h_lo_ready, 1)

                for c in range(4):
                    if c >= 2:
                        dve.wait_ge(h_lo_ready, 16 * n + 4 * (c - 1))
                    for k in range(4 * c, 4 * c + 4):
                        STT(out=(wc, wd)[c % 2][:, k % 4, :], in0=x[:, k, :], scalar=coef[:, k:k + 1], in1=rinv[:],
                            op0=MUL, op1=MUL).then_inc(ht_ready, 1)
                    if c:
                        rest(c - 1)
                rest(3)

            def mark_x(n):
                dve.memset(small[:, n:n + 1], 0.0).then_inc(x_ok, 1)

            def add_gated(J, c, gate, i=None):
                count = J // 3 if i is None else i * 2 + J // 3
                if i is not None:
                    dve.wait_ge(evac[J % 3], count - 1)
                elif J > J_MLA - 6:
                    dve.wait_ge(evac[J % 3], count)
                for m in range(4):
                    k = 4 * c + m
                    ins = STT(out=x[:, k, :], in0=pair(J)[:, m, :], scalar=modc[:, gate + k:gate + k + 1], in1=x[:, k, :],
                              op0=MUL, op1=ADD)
                ins.then_inc(evac[J % 3], 1)

            splits(0, 2)
            dve.wait_ge(S("cact"), 1)
            for hp in range(4):
                for m in range(8 * hp, 8 * hp + 8):
                    mod_unit(m)
                if hp:
                    mod_out(hp - 1)
            mod_out(3)
            for n in range(10):
                ins = dve.tensor_copy(ctab[:, n, :], cact[:, 0 if n < 2 else 16:][:, 0:16])
            ins.then_inc(S("ctab"), 1)
            dve.wait_ge(modc_ready, 4)
            mod_unit(32)
            mod_unit(33)
            rinverse(0)
            make_h(0, 16, "norm_attn")

            def split_mod(a, b):
                for u in range(a, b):
                    split(u)
                    mod_unit(32 + u)

            split_mod(2, 10)
            dve.wait_ge(S("c_root"), 1)
            dve.wait_ge(ht_ready, 16)
            dve.reciprocal(rinv[:], rs[:]).then_inc(S("c_rinv"), 1)
            dve.wait_ge(S("c_rinv"), 1)
            for k in range(2):
                STT(out=g6[:, 2 + k, :], in0=g6[:, 2 + k, :], scalar=c0("kv_norm", k), in1=rinv[:], op0=MUL, op1=MUL)\
                    .then_inc(S("c_norm"), 1)
            for k in range(2):
                dve.wait_ge(S("c_hi"), k + 1)
                TT(c_lo[:, k, :], g6[:, 2 + k, :], c_hi[:, k, :].bitcast(F32), SUB).then_inc(S("c_lo"), 1)
            split_mod(10, 16)
            dve.wait_ge(S("turned_out"), 1)
            for it in range(12):
                dve.wait_ge(S("idx_relu"), it + 1)
                for s, h in enumerate(idx_heads(it)):
                    b, n = (1, T) if it < 8 else (0, P)
                    o = isc[:, 0:T] if it < 8 else isc[:, T:T + P]
                    r = relu[:, it % 4, n * s:n * s + n]
                    done = 2 * it + s if it < 8 else 4 * it - 16 + s
                    if h == 0:
                        TS(o, r, wtok[:, b, h:h + 1], None, MUL).then_inc(S("idx_sum"), 1)
                    else:
                        dve.wait_ge(S("idx_sum"), done)
                        STT(out=o, in0=r, scalar=wtok[:, b, h:h + 1], in1=o, op0=MUL, op1=ADD).then_inc(S("idx_sum"), 1)
            dve.wait_ge(S("idx_sum"), 32)
            TT(isc[:], isc[:], k0_("causal3", 384), ADD).then_inc(S("isc"), 1)
            dve.wait_ge(S("isc"), 1)
            split_mod(16, 17)
            for r in range(TOPK // 8):
                for b, (c, w) in enumerate(((0, T), (T, P))):
                    if r:
                        dve.wait_ge(S("top_taken"), 2 * r - 1 + b)
                    dve.max(tiny[:, 64 + 8 * b:72 + 8 * b], isc[:, c:c + w]).then_inc(S("top_max"), 1)
                for b, (c, w) in enumerate(((0, T), (T, P))):
                    dve.wait_ge(S("top_max"), 2 * r + 1 + b)
                    dve.match_replace(isc[:, c:c + w], tiny[:, 64 + 8 * b:72 + 8 * b], isc[:, c:c + w], TAKEN)\
                        .then_inc(S("top_taken"), 1)
                split_mod(17 + r, 18 + r)
                if r == 1:
                    mod_out(4)
            dve.wait_ge(S("top_taken"), 2 * (TOPK // 8))
            TS(sel[:], isc[:], TAKEN, -NEG, ALU.is_equal, MUL).then_inc(S("sel"), 1)
            dve.wait_ge(S("sel"), 1)
            TS(sel[:], sel[:], NEG, None, ADD).then_inc(S("sel"), 1)
            split_mod(25, 26)
            mod_out(5)
            split_mod(26, 32)
            mod_out(6)

            def attention(a):
                sr, tn = (sring, tiny) if a < 2 else (sring2, tiny2)
                scale = 64 ** -0.5 if a < 2 else 192 ** -0.5
                for k in range(HEADS + 6):
                    n = 16 * a + k
                    if k < HEADS:
                        q = n % 4
                        dve.wait_ge(att_scores, n + 1)
                        if a == 0:
                            dve.wait_ge(bias_full[n % 3], 32 * (n // 3 + 1))
                        if a == 1:
                            dve.wait_ge(bias_sum, k + 1)
                        if n >= 4:
                            dve.wait_ge(att_turned, n - 3)
                        STT(out=sr[:, q, :], in0=ps[:, n % 3, 0:384], scalar=scale,
                            in1=bring[:, n % 3, :] if a < 2 else k0_("causal3", 384), op0=MUL, op1=ADD).then_inc(att_sc, 1)
                        dve.wait_ge(att_sc, n + 1)
                        if n >= 4:
                            dve.wait_ge(att_negm, n - 3)
                        dve.tensor_reduce(tn[:, 16 + 2 * q:17 + 2 * q], sr[:, q, 0:T], AX, ALU.max).then_inc(att_max, 1)
                        dve.tensor_reduce(tn[:, 17 + 2 * q:18 + 2 * q], sr[:, q, T:384], AX, ALU.max).then_inc(att_max, 1)
                    if 1 <= k <= HEADS:
                        m = n - 1
                        q = m % 4
                        dve.wait_ge(att_exp, exp_count(m + 1))
                        if m >= 4:
                            dve.wait_ge(att_prob, 2 * (m - 3))
                        if a == 0:
                            TT(tn[:, 48 + 2 * q:50 + 2 * q], tn[:, 32 + 2 * q:34 + 2 * q], tn[:, 40 + 2 * q:42 + 2 * q], ADD)\
                                .then_inc(att_den, 1)
                            dve.wait_ge(att_den, m + 1)
                        src = 48 if a == 0 else 32
                        dve.reciprocal(tn[:, 56 + 2 * q:58 + 2 * q], tn[:, src + 2 * q:src + 2 + 2 * q]).then_inc(att_rden, 1)
                    if k < HEADS:
                        q = n % 4
                        dve.wait_ge(att_max, 2 * n + 2)
                        if n >= 4:
                            dve.wait_ge(att_exp, exp_count(n - 3))
                        if a == 0:
                            h = order(a, k)
                            TS(tn[:, 24 + 2 * q:26 + 2 * q], tn[:, 16 + 2 * q:18 + 2 * q], tn[:, h:h + 1], -1.0, ALU.max, MUL)\
                                .then_inc(att_negm, 1)
                        else:
                            TS(tn[:, 24 + 2 * q:26 + 2 * q], tn[:, 16 + 2 * q:18 + 2 * q], -1.0, None, MUL).then_inc(att_negm, 1)
                    if a < 2 and k >= 6 and k % 2 == 0 and (k - 6) // 2 < 8:
                        j = (k - 6) // 2
                        dve.wait_ge(att_ohi, 8 * a + j + 1)
                        TT(h_lo[:, 8 * a + j, :], ps[:, 5 + 2 * (j % 2), 0:T], h_hi[:, 8 * a + j, :].bitcast(F32), SUB)\
                            .then_inc(att_olo, 1)
                    if a == 2:
                        if 4 <= k < HEADS + 4:
                            j = k - 4
                            dve.wait_ge(att_pv, n - 4 + 1)
                            TT(zs[:, j, :], ps[:, 5 + 2 * (j % 2), 0:T], zs[:, j, :], MUL).then_inc(att_o, 1)
                        if 5 <= k < HEADS + 5:
                            j = k - 5
                            dve.wait_ge(att_ohi, 16 + j + 1)
                            TT(h_lo[:, j, :], zs[:, j, :], h_hi[:, j, :].bitcast(F32), SUB).then_inc(att_olo, 1)

            attention(0)
            attention(1)
            split_mod(32, 38)
            job_done(12)
            add_gated(12, 0, 32)
            split_mod(38, 42)
            mod_out(7)
            job_done(13)
            add_gated(13, 1, 32)
            split_mod(42, 46)
            job_done(14)
            add_gated(14, 2, 32)
            split_mod(46, 48)
            mod_out(8)
            splits(48, 50)
            job_done(15)
            add_gated(15, 3, 32)
            mark_x(0)
            mod_out(9)
            dve.wait_ge(x_ok, 1)
            dve.wait_ge(modc_ready, 10)
            rinverse(1)
            make_h(1, 64, "norm_ffn")

            def convolve(s, i, channels):
                J = J_FF if i is None else J_FF + 2
                if i is None:
                    dve.tensor_copy(cwi[:], c0("conv", 0, 16)).then_inc(S("cwi"), 1)
                else:
                    dve.wait_ge(S("silu"), 4 * s)
                    dve.wait_ge(S("conv"), 12 * s)
                    dve.tensor_copy(cwi[:], col[:, bass.ds(s * 16 + COLS["conv"], 16)]).then_inc(S("cwi"), 1)
                dve.wait_ge(S("cwi"), s + 1)
                dve.wait_ge(evac[J % 3], channels)
                for j in range(3):
                    for m in range(4):
                        if j == 0:
                            TS(wa[:, m, :], ubuf[:, m, 2:2 + T], cwi[:, 3 * m + 2:3 * m + 3], None, MUL).then_inc(S("conv"), 1)
                        else:
                            dve.wait_ge(S("conv"), s * 12 + 4 * j - 3 + m)
                            STT(out=wa[:, m, :], in0=ubuf[:, m, 2 - j:2 - j + T], scalar=cwi[:, 3 * m + 2 - j:3 * m + 3 - j],
                                in1=wa[:, m, :], op0=MUL, op1=ADD).then_inc(S("conv"), 1)

            def gate_y(s, used):
                dve.wait_ge(half_used, used)
                dve.wait_ge(S("silu"), 4 * s + 4)
                if s is not ZERO:
                    dve.wait_ge(S("y_lo"), s)
                TT(wc[:], wb[:], pair(J_FF + 1), MUL).then_inc(S("y"), 1)

            def y_rest(s, rounded, J):
                dve.wait_ge(evac[J % 3], rounded)
                TT(y_lo[:], wc[:], y_hi[:].bitcast(F32), SUB).then_inc(S("y_lo"), 1)

            def add_part(J, c, i=None):
                dve.wait_ge(evac[J % 3], J // 3 - 1 if i is None else i * 2 + J // 3 - 1)
                TT(facc[:, 4 * c:4 * c + 4, :], pair(J), facc[:, 4 * c:4 * c + 4, :], ADD).then_inc(evac[J % 3], 1)

            splits(50, 54)
            dve.memset(ubuf[:, :, 0:2], 0.0).then_inc(S("zeroed"), 1)
            dve.memset(facc[:], 0.0).then_inc(S("facc_zero"), 1)
            dve.wait_ge(S("facc_zero"), 1)
            convolve(0, None, J_FF // 3 + 1)
            splits(54, 56)
            dve.wait_ge(S("ctab"), 1)
            with dve.Fori(0, FF_STEPS - 1) as i:
                dve.wait_ge(mod_sum, i * 16 + 160)
                dve.tensor_copy(cuse[:], ctab[:, bass.ds(i, 1), :].rearrange("p a n -> p (a n)")).then_inc(S("cuse"), 1)
                for k in range(12):
                    split(56 + k, i)
                    if k == 0:
                        dve.wait_ge(S("cuse"), i + 1)
                    if k < 8:
                        mod_unit(80 + k, i, c=cuse, two=False)
                    if k == 1:
                        gate_y(i, i * 24 + 2 * 56)
                        y_rest(i, i * 2 + (J_FF + 1) // 3 + 1, J_FF + 1)
                    if k == 5:
                        convolve(i + 1, i, i * 2 + (J_FF + 2) // 3 + 1)
                    if 6 <= k < 10:
                        dve.wait_ge(half_used, i * 24 + 2 * (61 + k - 6))
                        add_part(J_FF + 3 + k - 6, k - 6, i)
                    if k == 11:
                        mod_out(10, i)
            gate_y(FF_STEPS - 1, 2 * (U_V - 4))
            y_rest(FF_STEPS - 1, (FF_STEPS - 1) * 2 + (J_FF + 1) // 3 + 1, J_FF + 1)
            splits(U_V - 4, U_V - 2)
            for c in range(4):
                splits(U_V - 2 + c, U_V - 1 + c)
                job_done(J_V - 4 + c)
                add_part(J_V - 4 + c, c)
            for b in range(3):
                dve.wait_ge(evac[b], len([j for j in range(J_V) if j % 3 == b]))
            for k in range(KT):
                STT(out=x[:, k, :], in0=facc[:, k, :], scalar=modc[:, 80 + k:81 + k], in1=x[:, k, :], op0=MUL, op1=ADD)
            mark_x(1)
            dve.wait_ge(x_ok, 2)
            rinverse(2)
            for k in range(KT):
                STT(out=x[:, k, :], in0=x[:, k, :], scalar=c0("norm_final", k), in1=rinv[:], op0=MUL, op1=MUL)
            mark_x(2)
            dve.wait_ge(x_ok, 3)
            rinverse(3)
            make_h(2, 112, "norm_a")

            def moments(g):
                dve.wait_ge(evac[(J_V + g) % 3], (J_V + g) // 3 + 1)
                for t in range(2):
                    dve.bn_stats(stats[:, t, g, :], v[:, t, 512 * g:512 * g + 512]).then_inc(S("moments"), 1)

            for g in range(8):
                for k in range(4):
                    u = U_V + 4 * g + k
                    if u >= U_V + 2:
                        split(u)
                    if g and k == 1:
                        moments(g - 1)
                mod_unit(160 + g, two=False)
            splits(U_GM, U_GM + 2)
            moments(7)
            dve.wait_ge(S("moments"), 16)
            for t in range(2):
                ins = dve.bn_aggr(mv[:, t, :], stats[:, t, :, :])
            ins.then_inc(S("v_var"), 1)
            dve.wait_ge(S("v_root"), 1)
            dve.reciprocal(rstd[:], rstd[:]).then_inc(S("rstd"), 1)
            dve.wait_ge(S("rstd"), 1)
            dve.wait_ge(S("v_var"), 1)
            for t in range(2):
                TS(v[:, t, :], v[:, t, :], mv[:, t, 0:1], rstd[:, t:t + 1], SUB, MUL).then_inc(S("v_norm"), 1)
            splits(U_GM + 2, U_GM + 6)
            mod_out(20)
            splits(U_GM + 6, U_GM + 8)

            def gm_gate(s, used):
                J = J_GM + 1
                dve.wait_ge(S("tanh"), s + 1)
                dve.wait_ge(half_used, used)
                STT(out=wb[:], in0=wb[:], scalar=1.0, in1=pair(J), op0=ADD, op1=MUL).then_inc(S("gm_a"), 1)
                dve.wait_ge(S("gm_a"), 2 * s + 1)
                TT(wb[:], wb[:], wa[:], MUL).then_inc(S("gm_a"), 1)
                dve.wait_ge(S("wmix"), s + 1)
                dve.wait_ge(S("y_lo"), s + FF_STEPS)
                for g in range(2):
                    TT(wc[:].rearrange("p (g c) t -> p g (c t)", g=2)[:, g, :].rearrange("p (a t) -> p a t", a=4),
                       ps[:, 6 + g, :].rearrange("p (a t) -> p a t", a=4),
                       bsrow[:, g:g + 1, :].to_broadcast([P, 4, P]), ADD).then_inc(S("mixed"), 1)
                dve.wait_ge(S("mixed"), s * 2 + 2)
                dve.wait_ge(S("gm_a"), 2 * s + 2)
                STT(out=wc[:], in0=wc[:], scalar=0.5, in1=wb[:], op0=MUL, op1=MUL).then_inc(S("y"), 1)

            for b in range(3):
                dve.wait_ge(evac[b], len([j for j in range(J_GM) if j % 3 == b]))
            with dve.Fori(0, GM_STEPS - 1) as i:
                for k in range(12):
                    split(U_GM + 8 + k, i)
                    if k < 8:
                        mod_unit(168 + k, i, two=False)
                    if k == 1:
                        gm_gate(i, i * 24 + 2 * (U_GM + 8))
                        y_rest(i, i * 2 + (J_GM + 1) // 3 + 1, J_GM + 1)
                    if 6 <= k < 10:
                        dve.wait_ge(half_used, i * 24 + 2 * (U_GM + 13 + k - 6))
                        add_gated(J_GM + 3 + k - 6, k - 6, 128, i)
                    if k == 11:
                        mod_out(21, i)
            gm_gate(GM_STEPS - 1, 2 * (U_MLA - 4))
            y_rest(GM_STEPS - 1, (GM_STEPS - 1) * 2 + (J_GM + 1) // 3 + 1, J_GM + 1)
            splits(U_MLA - 4, U_MLA - 2)
            for c in range(4):
                splits(U_MLA - 2 + c, U_MLA - 1 + c)
                job_done(J_MLA - 4 + c)
                add_gated(J_MLA - 4 + c, c, 128)
            mark_x(3)
            dve.wait_ge(x_ok, 4)
            rinverse(4)
            U, J = U_MLA, J_MLA
            make_h(3, 160, "norm_kv")
            splits(U + 2, U + 8)

            def inverse(e, n):
                side = (wc, wd)[e % 2][:].rearrange("p a t -> p (a t)")[:, 0:n]
                dve.wait_ge(S("n_root"), e + 1)
                dve.reciprocal(side, side).then_inc(S("n_rinv"), 1)
                dve.wait_ge(S("n_rinv"), e + 1)
                return (wc, wd)[e % 2]

            def latent(e, j, buf, norm):
                r = inverse(e, T)
                for k in range(4):
                    STT(out=buf[:, k, :], in0=buf[:, k, :], scalar=c0(norm, k), in1=r[:, 0, :], op0=MUL, op1=MUL)\
                        .then_inc(S("n_c"), 1)
                dve.wait_ge(S("n_c"), 4 * j + 4)
                dve.memset(small[:, 8 + e:9 + e], 0.0).then_inc(S("n_used"), 1)

            def latent_rest(j, buf):
                for k in range(4):
                    dve.wait_ge(S("m_hi"), 4 * j + k + 1)
                    TT(m_lo[:, k, :], buf[:, k, :], m_hi[:, k, :].bitcast(F32), SUB).then_inc(S("m_lo"), 1)

            latent(0, 0, kn, "g_kva")
            r = inverse(1, T)
            STT(out=kr[:], in0=pair(J + 1)[:, 0, :], scalar=c0("g_kr"), in1=r[:, 0, :], op0=MUL, op1=MUL).then_inc(S("kr"), 1)
            STT(out=r[:, 1, :], in0=pair(J + 1)[:, 1, :], scalar=c0("g_krs"), in1=r[:, 0, :], op0=MUL, op1=MUL).then_inc(evac[(J + 1) % 3], 1)
            dve.wait_ge(evac[(J + 1) % 3], (J + 1) // 3 + 1)
            dve.wait_ge(S("kr"), 1)
            TT(kr[:], kr[:], k0_("cos", T), MUL).then_inc(S("kr"), 1)
            TT(r[:, 1, :], r[:, 1, :], k0_("sin", T), MUL).then_inc(S("kr"), 1)
            dve.wait_ge(S("kr"), 3)
            TT(kr[:], kr[:], r[:, 1, :], ADD).then_inc(S("n_used"), 1)
            latent_rest(0, kn)
            dve.wait_ge(S("n_used"), 2)
            make_h(4, 192, "norm_b")

            def normed(e, J, out_, norm):
                r = inverse(e, 1024)
                STT(out=out_, in0=pair(J), scalar=c0(norm), in1=r[:], op0=MUL, op1=MUL).then_inc(evac[J % 3], 1)
                dve.memset(small[:, 8 + e:9 + e], 0.0).then_inc(S("n_used"), 1)

            dve.wait_ge(S("m_lo"), 4)
            for k in range(4):
                splits(U + 8 + k, U + 9 + k)
                normed(2 + k, J + 2 + k, kn[:, 4 * k:4 * k + 4, :], "g_kn")
            splits(U + 12, U + 24)
            latent(6, 1, qr, "g_qa")
            latent_rest(1, qr)
            splits(U + 24, U + 37)
            for k in range(4):
                normed(7 + k, J + 15 + k, qn[:, 4 * k:4 * k + 4, :], "g_qn")
                splits(U + 37 + k, U + 38 + k)
            for k in range(2):
                r = inverse(11 + k, 1024)
                STT(out=qr[:, 4 * k:4 * k + 4, :], in0=pair(J + 19 + k), scalar=c0("g_qr"), in1=r[:], op0=MUL, op1=MUL)\
                    .then_inc(evac[(J + 19 + k) % 3], 1)
                splits(U + 41 + k, U + 42 + k)
            for k in range(2):
                r = (wd, wc)[k]
                job_done(J + 21 + k)
                dve.wait_ge(evac[(J + 19 + k) % 3], (J + 19 + k) // 3 + 1)
                q4 = qr[:, 4 * k:4 * k + 4, :]
                STT(out=r[:], in0=pair(J + 21 + k), scalar=c0("g_qrs"), in1=r[:], op0=MUL, op1=MUL)\
                    .then_inc(evac[(J + 21 + k) % 3], 1)
                dve.wait_ge(evac[(J + 21 + k) % 3], (J + 21 + k) // 3 + 1)
                TT(r[:], r[:], con[:, CST["sin"]:CST["sin"] + T].unsqueeze(1).to_broadcast([P, 4, T]), MUL).then_inc(S("qr"), 1)
                TT(q4, q4, con[:, CST["cos"]:CST["cos"] + T].unsqueeze(1).to_broadcast([P, 4, T]), MUL).then_inc(S("qr"), 1)
                dve.wait_ge(S("qr"), 2 * k + 2)
                TT(q4, q4, r[:], ADD).then_inc(S("qr_done"), 1)
            attention(2)
            splits(U + 43, U + 46)
            for k in range(4):
                splits(U + 46 + 4 * k, min(U + 50 + 4 * k, UNITS))
                job_done(J + 23 + k)
                add_gated(J + 23 + k, k, 208)
            mark_x(4)

        @block.gpsimd
        def _(pool):
            def normalize(a, n):
                sr, tn = (sring, tiny) if a < 2 else (sring2, tiny2)
                pool.wait_ge(att_rden, n + 1)
                for b, (c, w) in enumerate(((0, T), (T, P))):
                    pool.tensor_scalar(sr[:, n % 4, c:c + w], sr[:, n % 4, c:c + w],
                                       tn[:, 56 + 2 * (n % 4) + b:57 + 2 * (n % 4) + b], None, ALU.mult).then_inc(att_prob, 1)

            for n in range(16):
                normalize(0, n)
            pool.wait_ge(S("sel"), 2)
            for k in range(17):
                if k < 16:
                    pool.wait_ge(bias_full[(16 + k) % 3], 32 * ((16 + k) // 3 + 1))
                    b = bring[:, (16 + k) % 3, :]
                    pool.tensor_tensor(b, b, sel[:], ALU.add).then_inc(bias_sum, 1)
                if k >= 1:
                    normalize(1, 15 + k)

            def values(s):
                pool.wait_ge(S("lnrow"), s * 16 + 16)
                if s is not ZERO:
                    pool.wait_ge(S("wmix"), s)
                for t in range(2):
                    pool.tensor_tensor(vs[:, t, :], v[:, t, bass.ds(s * 512, 512)], lnrow[:, 0, :], ALU.mult).then_inc(S("vs_g"), 1)
                pool.wait_ge(S("wst"), s * 16 + 16)
                for g in range(2):
                    ins = pool.tensor_tensor(wst[:, g, :], wst[:, g, :], k0_("triu", P), ALU.mult)
                ins.then_inc(S("wst_masked"), 1)
                pool.wait_ge(S("vs_g"), s * 2 + 2)
                for t in range(2):
                    pool.tensor_tensor(vs[:, t, :], vs[:, t, :], lnrow[:, 1, :], ALU.add).then_inc(S("vs"), 1)

            pool.wait_ge(S("v_norm"), 2)
            values(ZERO)
            with pool.Fori(1, GM_STEPS) as i:
                values(i)
            for n in range(32, 48):
                normalize(2, n)


def _tiles(w):
    return w.reshape(w.shape[0] // P, P, w.shape[1])


def _units(w, width):
    k = 2048 // width
    t = w.reshape(w.shape[0] // (k * P), k, P, width).transpose(0, 2, 1, 3)
    return t.reshape(-1, P, 2048)


def _columns(vec):
    return vec.reshape(-1, P).T


def _shape_constants():
    import math
    con = np.zeros((P, NCST), np.float32)
    i, j = np.arange(P)[:, None], np.arange(P)[None, :]
    con[:, CST["ident"]:][:, :P] = i == j
    causal = np.where(j <= i, 0, NEG)
    con[:, CST["causal3"]:][:, P:384] = np.concatenate([causal, causal], 1)
    con[:, CST["triu"]:][:, :P] = i <= j
    con[:, CST["blk"]:][:, :P] = i // 64 == j // 64
    pos = np.arange(T, dtype=np.float32)
    freq = np.float32(10000.0) ** (-np.arange(0, 64, 2, dtype=np.float32) / np.float32(64))
    ang = (pos[:, None] * freq[None, :]).astype(np.float32).T
    con[:, CST["cos"]:][:, :T] = np.concatenate([np.cos(ang)] * 4, 0)
    con[:, CST["sin"]:][:, :T] = np.concatenate([-np.sin(ang), np.sin(ang)] * 2, 0)
    dist = 255 - np.arange(384)
    n = np.maximum(dist, 0)
    nf = np.maximum(n, 1).astype(np.float32)
    large = 16 + (np.log(nf / np.float32(16)) / np.float32(math.log(128 / 16)) * np.float32(16)).astype(np.int32)
    bucket = np.where(n < 16, n, np.minimum(large, 31))
    hot = np.zeros((33, 2, 384), np.float32)
    window = [(dist >= 0) & (dist < 128), dist >= 0]
    for a in range(2):
        hot[bucket[window[a]], a, np.nonzero(window[a])[0]] = 1
        hot[32, a] = np.where(window[a], 0, NEG)
    return con, hot.reshape(33, 768)


def kernel(x, c, w_mod, b_mod, norm_attn, w_in, attn_sinks, kv_norm, w_uk, w_uv, rel_bias, w_out,
           norm_ffn, w_up, conv_w, conv_b, w_down, norm_final, c_2, ada_w_2, ada_b_2, norm_g_2,
           a_w_in_2, a_ln_g_2, a_ln_b_2, a_w_s_2, a_b_s_2, a_w_out_2, kv_ada_w_2, kv_ada_b_2,
           kv_norm_g_2, kv_w_dkv_2, kv_g_kva_2, kv_w_ukv_2, kv_g_kn_2, kv_g_kr_2, b_w_in_2, b_g_qa_2,
           b_w_uq_2, b_g_qn_2, b_g_qr_2, b_w_out_2):
    import concourse.bacc as bacc
    from concourse.bass_utils import run_bass_kernel_spmd

    (x, c, w_mod, b_mod, norm_attn, w_in, attn_sinks, kv_norm, w_uk, w_uv, rel_bias, w_out,
     norm_ffn, w_up, conv_w, conv_b, w_down, norm_final, c_2, ada_w_2, ada_b_2, norm_g_2,
     a_w_in_2, a_ln_g_2, a_ln_b_2, a_w_s_2, a_b_s_2, a_w_out_2, kv_ada_w_2, kv_ada_b_2,
     kv_norm_g_2, kv_w_dkv_2, kv_g_kva_2, kv_w_ukv_2, kv_g_kn_2, kv_g_kr_2, b_w_in_2, b_g_qa_2,
     b_w_uq_2, b_g_qn_2, b_g_qr_2, b_w_out_2) = [np.asarray(a) for a in (
         x, c, w_mod, b_mod, norm_attn, w_in, attn_sinks, kv_norm, w_uk, w_uv, rel_bias, w_out,
         norm_ffn, w_up, conv_w, conv_b, w_down, norm_final, c_2, ada_w_2, ada_b_2, norm_g_2,
         a_w_in_2, a_ln_g_2, a_ln_b_2, a_w_s_2, a_b_s_2, a_w_out_2, kv_ada_w_2, kv_ada_b_2,
         kv_norm_g_2, kv_w_dkv_2, kv_g_kva_2, kv_w_ukv_2, kv_g_kn_2, kv_g_kr_2, b_w_in_2, b_g_qa_2,
         b_w_uq_2, b_g_qn_2, b_g_qr_2, b_w_out_2)]

    w = w_in[0]
    qa, ka, va, qb, ckv, qi, ki, wi = np.split(w, [1024, 1152, 1280, 2304, 2560, 3584, 3648], axis=1)
    qa = qa.reshape(D, 2, 8, 64).transpose(0, 2, 1, 3).reshape(D, 1024)
    parts = [_units(np.concatenate([ka, ki, ki, ckv], 1), 512),
             _units(np.concatenate([va, wi, np.zeros((D, 112), w.dtype)], 1), 256)]
    parts += [_units(m[:, 512 * g:512 * g + 512], 512) for m in (qi, qa, qb) for g in range(2)]
    for m in (w_uk[0], w_uv[0]):
        m = m.transpose(1, 0, 2).reshape(256, 1024)
        parts.append(np.concatenate([m[:, :512].reshape(2, P, 512).transpose(1, 0, 2).reshape(P, 1024),
                                     m[:, 512:].reshape(2, P, 512).transpose(1, 0, 2).reshape(P, 1024)], 1)[None])
    m = np.concatenate([w_out[0][:1024].reshape(2, 8, 64, D).transpose(1, 0, 2, 3).reshape(1024, D), w_out[0][1024:]], 0)
    parts += [_units(m[:, 512 * g:512 * g + 512], 512) for g in range(4)]

    def up(m, s):
        return _units(m[:, 512 * s:512 * s + 512], 512)

    def down(m, s):
        return [_units(m[512 * s:512 * s + 512, 512 * g:512 * g + 512], 512) for g in range(4)]

    def mlp(a, b, m, steps):
        got = [up(a, 0), up(b, 0)]
        for s in range(1, steps):
            got += [up(a, s)] + down(m, s - 1) + [up(b, s)]
        return got + down(m, steps - 1)

    parts += mlp(w_up[0][:, :D_FF], w_up[0][:, D_FF:], w_down[0], FF_STEPS)
    u, v, z = (a_w_in_2[0][:, GM * n:GM * n + GM] for n in range(3))
    parts += [up(v, s) for s in range(GM_STEPS)] + mlp(u, z, a_w_out_2[0], GM_STEPS)
    w = kv_w_dkv_2
    parts.append(_units(w[:, :512], 512))
    r, rs = w[:, 512:], np.concatenate([w[:, 544:], w[:, 512:544]], 1)
    parts += [_units(np.concatenate([m, m], 1), P) for m in (r, rs)]
    w = kv_w_ukv_2.reshape(512, 16, 256)
    parts += [up(m, s) for m in (w[:, :, :P].reshape(512, 2048), w[:, :, P:].reshape(512, 2048)) for s in range(4)]
    parts += [up(b_w_in_2[0], s) for s in range(5)]
    w = b_w_uq_2[0].reshape(512, 16, 192)
    parts += [up(w[:, :, :P].reshape(512, 2048), s) for s in range(4)]
    r = w[:, :, P:]
    for m in (r, np.concatenate([r[:, :, 32:], r[:, :, :32]], 2)):
        parts += [up(m.reshape(512, 1024), s) for s in range(2)]
    parts += [up(b_w_out_2[0], s) for s in range(4)]
    stream = np.concatenate(parts, 0)
    assert stream.shape == (UNITS, P, 2048)

    mods = []
    for m in (w_mod[0], ada_w_2[0], kv_ada_w_2, ada_w_2[1]):
        for n in range(m.shape[1] // 1024):
            mods.append(_units(m[:, 1024 * n:1024 * n + 1024], 1024))
    mods = np.concatenate(mods, 0)

    conv = np.concatenate([conv_w[0].T, conv_b[0][:, None]], 1)
    conv = conv.reshape(FF_STEPS, 4, P, 4)
    conv = np.concatenate([conv[..., :3].transpose(2, 0, 1, 3).reshape(P, FF_STEPS, 12),
                           conv[..., 3].transpose(2, 0, 1).reshape(P, FF_STEPS, 4)], 2).reshape(P, -1)
    b_all = np.concatenate([b_mod[0], ada_b_2[0], kv_ada_b_2, ada_b_2[1]])

    def twice(g):
        return np.concatenate([g, g])

    def swapped(g):
        return np.concatenate([g[32:], g[:32]])

    cols = np.concatenate([_columns(m) for m in (b_all, norm_attn[0], norm_ffn[0], norm_final, norm_g_2[0], kv_norm_g_2,
                                                 norm_g_2[1])] + [conv] +
                          [_columns(m) for m in (kv_norm[0], kv_g_kva_2, b_g_qa_2[0], kv_g_kn_2, b_g_qn_2[0],
                                                 twice(kv_g_kr_2), twice(swapped(kv_g_kr_2)), twice(b_g_qr_2[0]),
                                                 twice(swapped(b_g_qr_2[0])), c[0], c_2[0])], 1)
    con, hot = _shape_constants()
    rowpar = np.concatenate([a_ln_g_2[0].reshape(8, 512), a_ln_b_2[0].reshape(8, 512), a_b_s_2[0].reshape(8, 256)], 1)
    wsT = a_w_s_2[0].transpose(0, 2, 1).reshape(8, 2, P, P).transpose(0, 2, 1, 3).reshape(8, P, 256)
    arrays = {"stream": stream, "mods": mods, "xT": x[0].T.reshape(KT, P, T).transpose(1, 0, 2), "cols": cols, "cst": con,
              "relb": rel_bias, "onehot": hot, "sinks": attn_sinks[0], "rowpar": rowpar, "wsT": wsT}
    arrays = {n: np.ascontiguousarray(a) for n, a in arrays.items()}

    nc = bacc.Bacc("TRN2", target_bir_lowering=False, num_devices=1)
    args = [nc.dram_tensor(n, a.shape, F32, kind="ExternalInput").ap() for n, a in arrays.items()]
    out = nc.dram_tensor("out", (P, KT, T), F32, kind="ExternalOutput").ap()
    build(nc, *args, out)
    got = run_bass_kernel_spmd(nc, [arrays], core_ids=[0]).results[0]["out"]
    return np.ascontiguousarray(np.asarray(got).transpose(2, 1, 0).reshape(1, T, D))
```

```python
from contextlib import ExitStack

import numpy as np
import concourse.bass as bass
from concourse import mybir

F32 = mybir.dt.float32
F32R = mybir.dt.float32r
ALU = mybir.AluOpType
ACT = mybir.ActivationFunctionType
AX = mybir.AxisListType.X

P = 128
T = 256
D = 2048
KT = D // P
EPS = 1e-6
NEG = -1e30
TAKEN = -3e38
TOPK = 64
D_FF = 5632
FF_STEPS = D_FF // 512
GM = 4096
GM_STEPS = GM // 512
MOD_A = 12
MOD_B = 22
MOD_COLS = 8 * MOD_A + 6 * MOD_B
HALVES = 4
SLOTS = 4

U_OUT, U_FF, U_V = 32, 48, 180
U_GM = U_V + 32
U_MLA = U_GM + 8 + (GM_STEPS - 1) * 12 + 4
J_OUT, J_FF = 12, 16
J_V = J_FF + 2 + (FF_STEPS - 1) * 6 + 4
J_GM = J_V + 8
J_MLA = J_GM + 2 + (GM_STEPS - 1) * 6 + 4
UNITS = U_MLA + 58

COLS = {}
_n = 0
for _name, _w in (("b_mod", MOD_COLS), ("norm_attn", 16), ("norm_ffn", 16), ("norm_final", 16),
                  ("norm_a", 16), ("norm_kv", 16), ("norm_b", 16), ("conv", 16 * FF_STEPS),
                  ("kv_norm", 2), ("g_kva", 4), ("g_qa", 4), ("g_kn", 1), ("g_qn", 1),
                  ("g_kr", 1), ("g_krs", 1), ("g_qr", 1), ("g_qrs", 1), ("c", 32)):
    COLS[_name] = _n
    _n += _w
NCOLS = _n
CST = {}
_n = 0
for _name, _w in (("ident", 128), ("causal3", 384), ("triu", 128), ("cos", 256), ("sin", 256), ("blk", 128)):
    CST[_name] = _n
    _n += _w
NCST = _n


def build(nc, stream, mods_a, mods_b, xT, cols, cst, relb, onehot, sinks, rowpar, wsT, out):
    with ExitStack() as ctx:
        sems = {}

        def S(name):
            if name not in sems:
                sems[name] = ctx.enter_context(nc.semaphore(name))
            return sems[name]

        BASE = 16512
        place = {"at": BASE}

        def sb(name, shape, dt=F32, at=None):
            n = 4 * int(np.prod(shape[1:]))
            if at is None:
                at = place["at"]
                place["at"] = at + (n + 31) // 32 * 32
            return nc.alloc_sbuf_tensor_at(name, shape, dt, offset=at)

        raw = sb("raw", [P, SLOTS, 2048])
        hi = sb("hi", [P, HALVES, 1024], F32R)
        lo = sb("lo", [P, HALVES, 1024], F32R)
        AT_MOD = place["at"]
        mraw = sb("mraw", [P, 2, 2, 1024])
        macc = sb("macc", [P, 2, 1024])
        mraw_b = sb("mraw_b", [P, 2, 2, 768], at=AT_MOD)
        macc_b = sb("macc_b", [P, 2, 768], at=AT_MOD + 12 * 1024)
        x = sb("x", [P, KT, T])
        AT_H = place["at"]
        h_hi = sb("h_hi", [P, KT, T], F32R)
        h_lo = sb("h_lo", [P, KT, T], F32R)
        col = sb("col", [P, NCOLS])
        con = sb("con", [P, NCST])
        ones = sb("ones", [P, P])
        cact = sb("cact", [P, 32])
        modc = sb("modc", [P, MOD_COLS])
        coef = sb("coef", [P, 16])
        rs = sb("rs", [P, T])
        rinv = sb("rinv", [P, T])
        small = sb("small", [P, 64])
        AT = place["at"]
        END = 229344

        def area(items):
            at, made = AT, []
            for name, shape, dt in items:
                made.append(sb(name, shape, dt, at=at))
                at += 4 * int(np.prod(shape[1:]))
            assert at <= END, (items[0][0], at - END)
            return made

        KB = 1024
        wa, wb, wc, wd = area([(n, [P, 4, T], F32) for n in ("wa", "wb", "wc", "wd")])
        g6, csq, c_hi, c_lo, qa, qb, qi, vb, vtok, wtok, bring, sring, pt, isc, sel, tiny = area([
            ("g6", [P, 4, T], F32), ("csq", [P, 2, T], F32), ("c_hi", [P, 2, T], F32R), ("c_lo", [P, 2, T], F32R),
            ("qa", [P, 8, T], F32), ("qb", [P, 8, T], F32), ("qi", [P, 8, T], F32), ("vb", [P, 2, 1024], F32),
            ("vtok", [P, 2, P], F32), ("wtok", [P, 2, 16], F32), ("bring", [P, 3, 384], F32),
            ("sring", [P, 4, 384], F32), ("pt", [P, 2, 384], F32), ("isc", [P, 384], F32),
            ("sel", [P, 384], F32), ("tiny", [P, 96], F32)])
        relu = sb("relu", [P, 4, 512], at=AT + 18 * KB)
        kb = sb("kb", [P, 8, T], at=AT + 26 * KB)
        at = AT + (42 + 1 + 4) * KB + 512
        va = sb("va", [P, T], at=at)
        wiT = sb("wiT", [16, T], at=at + KB)
        bvec = sb("bvec", [16, 2, 384], at=at + 2 * KB)
        rel33 = sb("rel33", [33, 32], at=at + 6 * KB)
        hot33 = sb("hot33", [33, 768], at=at + 6 * KB + 128)
        early = sb("early", [P, 4, 2, 1024], at=AT_H)
        early2 = sb("early2", [P, 2, 2, 1024], at=AT + 16 * KB)
        facc = sb("facc", [P, KT, T], at=AT + 16 * KB)
        ubuf = sb("ubuf", [P, 4, T + 2], at=AT + 32 * KB)
        cwi = sb("cwi", [P, 16], at=AT + 37 * KB)
        y_hi = sb("y_hi", [P, 4, T], F32R, at=AT + 53 * KB)
        y_lo = sb("y_lo", [P, 4, T], F32R, at=AT_MOD + 20 * KB)
        lnrow = sb("lnrow", [P, 2, 512], at=AT + 12 * KB)
        v = sb("v", [P, 2, GM], at=AT + 16 * KB)
        vs = sb("vs", [P, 2, 512], at=AT + 48 * KB)
        wst = sb("wst", [P, 2, P], at=AT + 52 * KB)
        bsrow = sb("bsrow", [P, 2, P], at=AT + 57 * KB)
        stats = sb("stats", [P, 2, 8, 6], at=AT + 58 * KB)
        mv = sb("mv", [P, 2, 2], at=AT + 58 * KB + 512)
        rstd = sb("rstd", [P, 2], at=AT + 58 * KB + 544)
        kn = sb("kn", [P, 16, T], at=AT + 16 * KB)
        vm = sb("vm", [P, 2, 2048], at=AT + 32 * KB)
        kr = sb("kr", [P, T], at=AT + 48 * KB)
        qr = sb("qr", [P, 8, T], at=AT + 49 * KB)
        tiny2 = sb("tiny2", [P, 96], at=AT + 57 * KB)
        sring2 = sb("sring2", [P, 4, 384], at=AT)
        pt2 = sb("pt2", [P, 2, 384], at=AT + 6 * KB)
        zs = sb("zs", [P, 16, T], at=AT_MOD)
        m_hi = sb("m_hi", [P, 4, T], F32R, at=AT_MOD + 16 * KB)
        m_lo = sb("m_lo", [P, 4, T], F32R, at=AT_MOD + 20 * KB)
        qn = sb("qn", [P, 16, T], at=AT_H)
        qrs = sb("qrs", [P, 4, T], at=AT_H + 16 * KB)

        ps = ctx.enter_context(nc.psum_tensor("ps", [P, 8, 512], F32))
        scratch = nc.dram_tensor("bias_rows", (2, 16, P, 384), F32)

        def pair(J):
            p = J % 3
            return ps[:, 2 * p:2 * p + 2, :].rearrange("p b (m t) -> p (b m) t", m=2)

        def pair2(J):
            p = J % 3
            return ps[:, 2 * p:2 * p + 2, :]

        def mod_slot(m):
            if m < 32:
                q = m % 8
                return (mraw[:, q, :, :] if q < 2 else early[:, q - 2, :, :] if q < 6 else early2[:, q - 6, :, :]), q
            return (mraw if m < 8 * MOD_A else mraw_b)[:, m % 2, :, :], m % 2

        def mod_turn(m):
            return m // 8 + 1 if m < 32 else 4 + (m - 32) // 2 + 1

        def mod_at(hp):
            return (8 * hp, 8) if hp < MOD_A else (8 * MOD_A + 6 * (hp - MOD_A), 6)

        def mod_acc(hp, i=None):
            return (macc if hp < MOD_A else macc_b)[:, hp % 2 if i is None else 0, :]

        def c0(name, k=0, n=1):
            return col[:, COLS[name] + k:COLS[name] + k + n]

        def k0_(name, n):
            return con[:, CST[name]:CST[name] + n]

        raw_full = [S(f"raw_full{i}") for i in range(SLOTS)]
        mod_full = [S(f"mod_full{i}") for i in range(8)]
        evac = [S(f"evac{i}") for i in range(3)]
        hi_ready = S("hi_ready")
        lo_ready = S("lo_ready")
        half_used = S("half_used")
        consts = S("consts")
        NCONST = 6
        mod_sum = S("mod_sum")
        colsum = S("colsum")
        modc_ready = S("modc_ready")
        x_ok = S("x_ok")
        sq_ready, stat_sum = S("sq_ready"), S("stat_sum")
        sq_added = S("sq_added")
        X_MARKS = {0: 0, 1: 0, 2: 4, 3: 9}
        root_ready, rinv_ready = S("root_ready"), S("rinv_ready")
        coef_ready, ht_ready = S("coef_ready"), S("ht_ready")
        h_hi_ready, h_lo_ready = S("h_hi_ready"), S("h_lo_ready")

        block = ctx.enter_context(nc.Block())

        SPAN = {}
        at_h = 0
        for J, n in enumerate([8, 4] + [8] * 6 + [1] * 4 + [8] * 4 + [8, 8]):
            SPAN[J] = (at_h, n)
            at_h += n
        for g in range(8):
            SPAN[J_V + g] = (2 * U_V + 8 * g, 8)
        SPAN[J_GM], SPAN[J_GM + 1] = (2 * U_GM, 8), (2 * U_GM + 8, 8)
        for c in range(4):
            SPAN[J_V - 4 + c] = (2 * U_V - 8 + 2 * c, 2)
            SPAN[J_MLA - 4 + c] = (2 * U_MLA - 8 + 2 * c, 2)
        at_h = 2 * U_MLA
        for J, n in enumerate([8, 4] + [2] * 8 + [8] * 5 + [2] * 8 + [8] * 4):
            SPAN[J_MLA + J] = (at_h, n)
            at_h += n
        assert at_h == 2 * UNITS

        def last_half(J):
            return SPAN[J][0] + SPAN[J][1]

        HEADS = 16
        att_scores, att_sc, att_max, att_negm = S("att_scores"), S("att_sc"), S("att_max"), S("att_negm")
        att_exp, att_den, att_rden, att_prob = S("att_exp"), S("att_den"), S("att_rden"), S("att_prob")
        att_turned, att_pt, att_pv = S("att_turned"), S("att_pt"), S("att_pv")
        att_o, att_ohi, att_olo = S("att_o"), S("att_ohi"), S("att_olo")
        bias_full = [S(f"bias_full{i}") for i in range(3)]
        bias_sum = S("bias_sum")

        def order(a, k):
            return (k // 2 + 8 * (k % 2)) if a == 0 else k

        def idx_ops(it):
            return 2 * (it + 1) if it < 8 else 16 + 4 * (it - 7)

        def idx_heads(it):
            return range(4 * (it // 2) + it % 2, 4 * (it // 2) + 4, 2) if it < 8 else \
                range(8 * (it // 2 - 4) + it % 2, 8 * (it // 2 - 4) + 8, 2)

        def exp_count(n):
            return 3 * min(n, 16) + 2 * max(0, n - 16)

        @block.sync
        def _(sp):
            def load(u, i=None, per=0):
                at = u if i is None else i * per + u
                if u >= SLOTS:
                    sp.wait_ge(lo_ready, 2 * (at - SLOTS) + 2)
                sp.dma_start(raw[:, u % SLOTS, :], stream[at]).then_inc(raw_full[u % SLOTS], 16)

            def load_mod(m, i=None, per=0):
                at = m if i is None else i * per + m
                back = 8 if m < 32 else 2
                if m in (32, 33):
                    sp.wait_ge(mod_sum, 2 * (m - 7))
                elif m >= back:
                    sp.wait_ge(mod_sum, 2 * (at - back + 1))
                slot, q = mod_slot(m)
                sp.dma_start(slot.rearrange("p k n -> p (k n)"), mods_a[at] if m < 8 * MOD_A else mods_b[at - 8 * MOD_A])\
                    .then_inc(mod_full[q], 16)

            sp.dma_start(col[:], cols).then_inc(consts, 16)
            for m in range(4):
                load_mod(m)
            sp.dma_start(tiny[:, 0:16], sinks.partition_broadcast(P)).then_inc(consts, 16)
            sp.dma_start(con[:], cst).then_inc(consts, 16)
            sp.dma_start(rel33[0:32, :], relb).then_inc(consts, 16)
            sp.dma_start(hot33[:], onehot).then_inc(consts, 16)
            sp.dma_start(x[:], xT).then_inc(consts, 16)
            for m in range(4, 8):
                load_mod(m)
            with sp.Fori(0, 2) as i:
                for m in range(8, 16):
                    load_mod(m, i, 8)
            load(0)
            load(1)
            for m in range(24, 32):
                load_mod(m)
            load(2)
            load(3)
            load_mod(32)
            load_mod(33)
            for u in range(2):
                load(4 + u)
            sp.wait_ge(S("bias_rows_ready"), 1)
            for a in range(2):
                sp.dma_start(scratch.ap()[a], bvec[:, a:a + 1, :].to_broadcast([16, P, 384])).then_inc(S("bias_rows"), 16)
            for m in range(34, 36):
                load_mod(m)
            with sp.Fori(0, 7) as i:
                for k in range(4):
                    load(6 + k, i, 4)
                    load_mod(36 + k, i, 4)
            for k in range(2):
                load(34 + k)
                load_mod(64 + k)
            sp.wait_ge(S("bias_rows"), 32)
            for n in range(2 * HEADS):
                a, h = n // HEADS, order(n // HEADS, n % HEADS)
                if n >= 3:
                    sp.wait_ge(att_sc, n - 2)
                for j, (c, w) in enumerate(((0, 256), (128, 128))):
                    sp.dma_start(bring[:, n % 3, 256 * j:256 * j + w],
                                 bass.AP(scratch, (a * 16 + h) * P * 384 + 127 + c, [[383, P], [1, w]]))\
                        .then_inc(bias_full[n % 3], 16)
                if n >= 4 and n % 2 == 0:
                    load_mod(66 + (n - 4) // 2)
            load_mod(80)
            load_mod(81)
            for k in range(14):
                load(36 + k)
                load_mod(82 + k)
            for k in range(10):
                load(50 + k)
            with sp.Fori(0, FF_STEPS - 1) as i:
                load_mod(96, i, 8)
                load_mod(97, i, 8)
                for k in range(12):
                    load(60 + k, i, 12)
                    if k < 6:
                        load_mod(98 + k, i, 8)
            load_mod(176)
            load_mod(177)
            with sp.Fori(0, 4) as i:
                for k in range(8):
                    load(U_V + k, i, 8)
                    load_mod(178 + k, i, 8)
            for k in range(8):
                load(U_GM + k)
                if k < 6:
                    load_mod(210 + k)
            for k in range(4):
                load(U_GM + 8 + k)

            def load_rows(s):
                sp.dma_start(lnrow[:].rearrange("p a n -> p (a n)"), rowpar[s, 0:1024].partition_broadcast(P))\
                    .then_inc(S("lnrow"), 16)
                sp.dma_start(bsrow[:].rearrange("p a n -> p (a n)"), rowpar[s, 1024:1280].partition_broadcast(P))\
                    .then_inc(S("bsrow"), 16)
                sp.dma_start(wst[:].rearrange("p a n -> p (a n)"), wsT[s]).then_inc(S("wst"), 16)

            sp.wait_ge(h_lo_ready, 16 * 3)
            sp.wait_ge(h_hi_ready, 16 * 3)
            load_rows(0)
            with sp.Fori(0, GM_STEPS - 1) as i:
                load_mod(216, i, 8)
                load_mod(217, i, 8)
                for k in range(12):
                    load(U_GM + 12 + k, i, 12)
                    if k < 6:
                        load_mod(218 + k, i, 8)
                    if k == 8:
                        sp.wait_ge(S("mixed"), 2 * (i + 1))
                        sp.wait_ge(S("wmix"), i + 1)
                        load_rows(i + 1)
            for k in range(UNITS - U_MLA):
                load(U_MLA + k)
            sp.wait_ge(x_ok, 14)
            sp.dma_start(out, x[:]).then_inc(S("stored"), 16)
            sp.wait_ge(S("stored"), 16)

        @block.scalar
        def _(act):
            act.wait_ge(consts, 16 * NCONST)

            def split(u, i=None):
                at = u if i is None else i * 12 + u
                act.wait_ge(raw_full[u % SLOTS], 16 * (u // SLOTS + 1) if i is None else i * 48 + 16 * (u // SLOTS + 1))
                for h in range(2):
                    if 2 * u + h >= HALVES:
                        act.wait_ge(half_used, 2 * at + h - HALVES + 1)
                    act.activation(hi[:, (2 * u + h) % HALVES, :], raw[:, u % SLOTS, 1024 * h:1024 * h + 1024],
                                   ACT.Copy).then_inc(hi_ready, 1)

            def splits(a, b):
                for u in range(a, b):
                    split(u)

            def job_done(J):
                act.wait_ge(half_used, last_half(J))

            def square_chunk(s, c):
                n = X_MARKS[s] + c + 1
                if s:
                    act.wait_ge(x_ok, n)
                    act.wait_ge(stat_sum, s)
                if c >= 2:
                    act.wait_ge(sq_added, 2 * s + c - 1)
                act.activation((wa if c == 0 else wb)[:], x[:, 4 * c:4 * c + 4, :], ACT.Square).then_inc(sq_ready, 1)
                if s == 2:
                    if c == 0:
                        act.wait_ge(S("y_lo"), FF_STEPS)
                    if c >= 2:
                        act.wait_ge(S("sq2_added"), c - 1)
                    for k in range(4):
                        ins = act.activation((wc if c == 0 else wd)[:, k, :], x[:, 4 * c + k, :], ACT.Square,
                                             scale=c0("norm_final", 4 * c + k))
                    ins.then_inc(S("sq2_ready"), 1)

            def x_root(s):
                act.wait_ge(stat_sum, s + 1)
                if s:
                    act.wait_ge(rinv_ready, s)
                    act.wait_ge(S("c_rinv"), 1)
                act.activation(rs[:], ps[:, 7, 0:T], ACT.Sqrt, scale=1.0 / D, bias=EPS).then_inc(root_ready, 1)

            def h_rounded(n, shift):
                for k in range(KT):
                    act.wait_ge(ht_ready, 16 * n + 4 * (k // 4) + 4)
                    act.activation(h_hi[:, k, :], (wc, wd)[(k // 4) % 2][:, k % 4, :], ACT.Identity,
                                   bias=modc[:, shift + k:shift + k + 1]).then_inc(h_hi_ready, 1)

            act.activation(cact[:], c0("c", 0, 32), ACT.Silu).then_inc(S("cact"), 1)
            act.wait_ge(S("bias_mm"), 2)
            act.activation(bvec[:, 0, :], ps[0:16, 6, 0:384], ACT.Copy)
            act.activation(bvec[:, 1, :], ps[0:16, 7, 0:384], ACT.Copy).then_inc(S("bias_rows_ready"), 1)
            for c in range(4):
                square_chunk(0, c)
            x_root(0)
            splits(0, 2)
            h_rounded(0, 0)
            splits(2, 6)
            job_done(0)
            act.activation(g6[:], pair(0), ACT.Copy).then_inc(evac[0], 1)
            act.wait_ge(evac[0], 1)
            act.activation(csq[:], g6[:, 2:4, :], ACT.Square).then_inc(S("c_sq"), 1)
            splits(6, 8)
            job_done(1)
            act.wait_ge(S("bias_rows"), 32)
            act.activation(va[:], pair(1)[:, 0, :], ACT.Copy)
            act.activation(wiT[:], pair(1)[0:16, 1, :], ACT.Copy, scale=64 ** -0.5 * 16 ** -0.5).then_inc(evac[1], 1)
            splits(8, 12)
            job_done(2)
            act.activation(qi[:, 0:4, :], pair(2), ACT.Copy).then_inc(evac[2], 1)
            act.wait_ge(S("c_sum"), 1)
            act.wait_ge(rinv_ready, 1)
            act.activation(rs[:], ps[:, 7, 0:T], ACT.Sqrt, scale=1.0 / 256, bias=EPS).then_inc(S("c_root"), 1)
            act.wait_ge(S("turned"), 1)
            act.activation(vtok[:], ps[:, 6, 0:256].rearrange("p (a c) -> p a c", a=2), ACT.Copy)
            act.activation(wtok[:], ps[:, 6, 256:288].rearrange("p (a c) -> p a c", a=2), ACT.Copy).then_inc(S("turned_out"), 1)
            for k in range(2):
                act.wait_ge(S("c_norm"), k + 1)
                act.activation(c_hi[:, k, :], g6[:, 2 + k, :], ACT.Copy).then_inc(S("c_hi"), 1)
            splits(12, 16)
            job_done(3)
            act.activation(qi[:, 4:8, :], pair(3), ACT.Copy).then_inc(evac[0], 1)
            for it in range(12):
                act.wait_ge(S("idx_mm"), it + 1)
                if it >= 4:
                    act.wait_ge(S("idx_sum"), idx_ops(it - 4))
                act.activation(relu[:, it % 4, :], ps[:, it % 4, :], ACT.Relu).then_inc(S("idx_relu"), 1)
            splits(16, 20)
            job_done(4)
            act.activation(qa[:, 0:4, :], pair(4), ACT.Copy).then_inc(evac[1], 1)
            splits(20, 24)
            job_done(5)
            act.activation(qa[:, 4:8, :], pair(5), ACT.Copy).then_inc(evac[2], 1)
            splits(24, 28)
            job_done(6)
            act.wait_ge(S("idx_sum"), 32)
            act.activation(qb[:, 0:4, :], pair(6), ACT.Copy).then_inc(evac[0], 1)
            splits(28, 32)
            job_done(7)
            act.activation(qb[:, 4:8, :], pair(7), ACT.Copy).then_inc(evac[1], 1)
            for j in range(2):
                job_done(8 + j)
                act.activation(kb[:, 4 * j:4 * j + 4, :], pair(8 + j), ACT.Copy).then_inc(evac[(8 + j) % 3], 1)
            for j in range(2):
                job_done(10 + j)
                act.activation(vb[:, :, 512 * j:512 * j + 512], pair2(10 + j), ACT.Copy).then_inc(evac[(10 + j) % 3], 1)

            def attention(a):
                sr, tn, pb = (sring, tiny, pt) if a < 2 else (sring2, tiny2, pt2)
                for k in range(HEADS + 4):
                    n = 16 * a + k
                    if k < HEADS:
                        act.wait_ge(att_negm, n + 1)
                        if n >= 4:
                            act.wait_ge(att_prob, 2 * (n - 3))
                        for b, (c, w) in enumerate(((0, 256), (256, 128))):
                            act.activation(sr[:, n % 4, c:c + w], sr[:, n % 4, c:c + w], ACT.Exp,
                                           bias=tn[:, 24 + 2 * (n % 4) + b:25 + 2 * (n % 4) + b],
                                           accum_out=tn[:, 32 + 2 * (n % 4) + b:33 + 2 * (n % 4) + b])\
                                .then_inc(att_exp, 1)
                        if a == 0:
                            h = order(a, k)
                            act.activation(tn[:, 40 + 2 * (n % 4):42 + 2 * (n % 4)],
                                           tn[:, 24 + 2 * (n % 4):26 + 2 * (n % 4)], ACT.Exp,
                                           bias=tn[:, h:h + 1]).then_inc(att_exp, 1)
                    if 3 <= k < HEADS + 3:
                        m = n - 3
                        act.wait_ge(att_turned, m + 1)
                        if a == 2 and k == 3:
                            act.wait_ge(S("qn_done"), 4)
                        if m >= 2:
                            act.wait_ge(att_pv, m - 1)
                        act.activation(pb[:, m % 2, :], ps[:, 3 + m % 2, 0:384], ACT.Copy).then_inc(att_pt, 1)
                    if k >= 4 and a < 2 and k % 2 == 1:
                        j = (k - 5) // 2
                        act.wait_ge(att_pv, 16 * a + 2 * j + 2)
                        act.activation(h_hi[:, 8 * a + j, :], ps[:, 5 + 2 * (j % 2), 0:T], ACT.Copy).then_inc(att_ohi, 1)
                    if k >= 4 and a == 2:
                        j = k - 4
                        act.wait_ge(att_o, j + 1)
                        act.activation(h_hi[:, j, :], zs[:, j, :], ACT.Copy).then_inc(att_ohi, 1)

            attention(0)
            attention(1)
            splits(32, 36)
            for c in range(4):
                splits(36 + 4 * c, min(40 + 4 * c, 50))
                square_chunk(1, c)
            x_root(1)
            h_rounded(1, 48)

            def channels_out(pos, s, J):
                act.wait_ge(half_used, pos)
                act.wait_ge(S("conv"), 12 * s)
                act.activation(ubuf[:, :, 2:2 + T], pair(J), ACT.Copy).then_inc(evac[J % 3], 1)

            def conv_silu(s, first_step=False):
                for m in range(4):
                    act.wait_ge(S("conv"), 12 * s + 9 + m)
                    if m == 0 and not first_step:
                        act.wait_ge(S("y"), s)
                    act.activation(wb[:, m, :], wa[:, m, :], ACT.Silu, bias=cwi[:, 12 + m:13 + m]).then_inc(S("silu"), 1)

            def y_rounded(s, used, J):
                act.wait_ge(S("y"), s + 1)
                act.wait_ge(half_used, used)
                act.activation(y_hi[:], wc[:], ACT.Copy).then_inc(evac[J % 3], 1)

            splits(50, 54)
            act.wait_ge(S("zeroed"), 1)
            act.wait_ge(half_used, last_half(J_FF))
            act.activation(ubuf[:, :, 2:2 + T], pair(J_FF), ACT.Copy).then_inc(evac[J_FF % 3], 1)
            conv_silu(0, first_step=True)
            splits(54, 56)
            with act.Fori(0, FF_STEPS - 1) as i:
                for k in range(12):
                    split(56 + k, i)
                    if k == 1:
                        y_rounded(i, i * 24 + 2 * 56, J_FF + 1)
                    if k == 5:
                        channels_out(i * 24 + 2 * 60, i + 1, J_FF + 2)
                    if k == 6:
                        conv_silu(i + 1)
            y_rounded(FF_STEPS - 1, 2 * (U_V - 4), J_FF + 1)
            splits(U_V - 4, U_V - 1)
            for c in range(4):
                splits(U_V - 1 + c, min(U_V + c, U_V + 2))
                square_chunk(2, c)
            act.wait_ge(S("ff_norm"), 3)
            act.activation(rs[:], rs[:], ACT.Sqrt)
            act.activation(rinv[:], rinv[:], ACT.Sqrt, bias=EPS).then_inc(root_ready, 1)
            h_rounded(2, 96)

            def v_out(pos, g, J):
                act.wait_ge(half_used, pos)
                for t in range(2):
                    ins = act.activation(v[:, t, bass.ds(g * 512, 512)], pair2(J)[:, t, :], ACT.Gelu_apprx_tanh)
                ins.then_inc(evac[J % 3], 1)

            splits(U_V + 2, U_V + 6)
            for g in range(8):
                job_done(J_V + g)
                for t in range(2):
                    ins = act.activation(v[:, t, 512 * g:512 * g + 512], pair2(J_V + g)[:, t, :], ACT.Gelu_apprx_tanh)
                ins.then_inc(evac[(J_V + g) % 3], 1)
                if g == 7:
                    act.wait_ge(S("v_var"), 1)
                    act.activation(rstd[:], mv[:, :, 1], ACT.Sqrt, bias=EPS).then_inc(S("v_root"), 1)
                    splits(U_V + 34, U_V + 38)
                else:
                    splits(U_V + 6 + 4 * g, U_V + 10 + 4 * g)

            def gelu_out(J, s):
                act.activation(wa[:], pair(J), ACT.Gelu_apprx_tanh).then_inc(evac[J % 3], 1)

            def tanh_out(J):
                act.activation(wb[:], pair(J), ACT.Tanh, scale=0.5).then_inc(S("tanh"), 1)

            job_done(J_GM)
            gelu_out(J_GM, 0)
            splits(U_V + 38, U_GM + 8)
            with act.Fori(0, GM_STEPS - 1) as i:
                for k in range(12):
                    split(U_GM + 8 + k, i)
                    if k == 1:
                        act.wait_ge(half_used, i * 24 + 2 * (U_GM + 8))
                        act.wait_ge(S("y"), FF_STEPS + i)
                        tanh_out(J_GM + 1)
                        act.wait_ge(S("y"), FF_STEPS + i + 1)
                        act.activation(y_hi[:], wc[:], ACT.Copy).then_inc(evac[(J_GM + 1) % 3], 1)
                    if k == 5:
                        act.wait_ge(half_used, i * 24 + 2 * (U_GM + 12))
                        gelu_out(J_GM + 2, i + 1)
            act.wait_ge(half_used, 2 * (U_MLA - 4))
            tanh_out(J_GM + 1)
            act.wait_ge(S("y"), FF_STEPS + GM_STEPS)
            act.activation(y_hi[:], wc[:], ACT.Copy).then_inc(evac[(J_GM + 1) % 3], 1)
            splits(U_MLA - 4, U_MLA - 1)
            for c in range(4):
                splits(U_MLA - 1 + c, min(U_MLA + c, U_MLA + 2))
                square_chunk(3, c)
            x_root(3)

            def root(e, wide, scale):
                act.wait_ge(S("n_sum"), e + 1)
                if e >= 11:
                    act.wait_ge(S("qn_done"), e - 10)
                elif e >= 2:
                    act.wait_ge(S("n_used"), e - 1)
                if e == 2:
                    act.wait_ge(h_lo_ready, 80)
                act.activation((wc, wd)[e % 2][:].rearrange("p a t -> p (a t)")[:, 0:wide],
                               ps[:, 6:8, :].rearrange("p b t -> p (b t)")[:, 0:wide], ACT.Sqrt,
                               scale=scale, bias=EPS).then_inc(S("n_root"), 1)

            def square(e, src, n):
                if e >= 2:
                    act.wait_ge(S("n_sum"), e - 1)
                act.activation((wa, wb)[e % 2][:, 0:n, :], src, ACT.Square).then_inc(S("n_sq"), 1)

            def c_rounded(j):
                for k in range(4):
                    act.wait_ge(S("n_c"), 4 * j + k + 1)
                    act.activation(m_hi[:, k, :], (kn, qr)[j][:, k, :], ACT.Copy).then_inc(S("m_hi"), 1)

            U, J = U_MLA, J_MLA
            h_rounded(3, 144)
            splits(U + 2, U + 6)
            job_done(J)
            act.activation(kn[:, 0:4, :], pair(J), ACT.Copy).then_inc(evac[J % 3], 1)
            act.wait_ge(evac[J % 3], J // 3 + 1)
            square(0, kn[:, 0:4, :], 4)
            root(0, T, 1 / 512)
            splits(U + 6, U + 7)
            c_rounded(0)
            splits(U + 7, U + 8)
            job_done(J + 1)
            square(1, pair(J + 1)[:, 0:1, :], 1)
            root(1, T, 1 / 64)
            h_rounded(4, 176)
            for k in range(4):
                keys, values = J + 2 + 2 * k, J + 3 + 2 * k
                splits(U + 8 + 2 * k, U + 9 + 2 * k)
                job_done(keys)
                square(2 + k, pair(keys), 4)
                if k == 0:
                    act.wait_ge(S("m_lo"), 4)
                act.activation(kn[:, 4 * k:4 * k + 4, :], pair(keys), ACT.Copy, scale=c0("g_kn")).then_inc(evac[keys % 3], 1)
                splits(U + 9 + 2 * k, U + 10 + 2 * k)
                job_done(values)
                act.activation(vm[:, :, 512 * k:512 * k + 512], pair2(values), ACT.Copy).then_inc(evac[values % 3], 1)
                root(2 + k, 1024, 1 / 128)
            splits(U + 16, U + 20)
            job_done(J + 10)
            act.activation(qr[:, 0:4, :], pair(J + 10), ACT.Copy).then_inc(evac[(J + 10) % 3], 1)
            act.wait_ge(evac[(J + 10) % 3], (J + 10) // 3 + 1)
            square(6, qr[:, 0:4, :], 4)
            splits(U + 20, U + 24)
            root(6, T, 1 / 512)
            c_rounded(1)
            for k in range(4):
                job_done(J + 11 + k)
                act.activation(zs[:, 4 * k:4 * k + 4, :], pair(J + 11 + k), ACT.Silu).then_inc(evac[(J + 11 + k) % 3], 1)
                splits(U + 24 + 4 * k, U + 28 + 4 * k) if k < 3 else splits(U + 36, U + 37)
            act.wait_ge(S("m_lo"), 8)
            for k in range(2):
                part, swapped = J + 15 + 2 * k, J + 16 + 2 * k
                job_done(part)
                square(7 + k, pair(part), 4)
                act.activation(qr[:, 4 * k:4 * k + 4, :], pair(part), ACT.Copy, scale=c0("g_qr")).then_inc(evac[part % 3], 1)
                splits(U + 37 + 2 * k, U + 38 + 2 * k)
                job_done(swapped)
                if k:
                    act.wait_ge(S("qr_sum"), 1)
                act.activation(qrs[:], pair(swapped), ACT.Copy, scale=c0("g_qrs")).then_inc(evac[swapped % 3], 1)
                root(7 + k, 1024, 1 / 64)
                splits(U + 38 + 2 * k, U + 39 + 2 * k)
            for k in range(4):
                job_done(J + 19 + k)
                square(9 + k, pair(J + 19 + k), 4)
                act.activation(qn[:, 4 * k:4 * k + 4, :], pair(J + 19 + k), ACT.Copy, scale=c0("g_qn"))\
                    .then_inc(evac[(J + 19 + k) % 3], 1)
                if k < 3:
                    splits(U + 41 + k, U + 42 + k)
                root(9 + k, 1024, 1 / 128)
            attention(2)
            splits(U + 44, UNITS)

        @block.tensor
        def _(pe):
            pe.wait_ge(consts, 16 * NCONST)
            pe.wait_ge(S("ones"), 2)

            def three(o, w_hi, w_lo, a_hi, a_lo, start, stop, weights_stay):
                for n, (w, a) in enumerate(((w_hi, a_hi), (w_hi, a_lo), (w_lo, a_hi))):
                    lhsT, rhs = (w, a) if weights_stay else (a, w)
                    ins = pe.matmul(o, lhsT, rhs, start=start and n == 0, stop=stop and n == 2, skip_group_check=True)
                return ins

            def job(J, a_hi, a_lo, k0=0, wide=512, turned=False, tiles=None, first=None, i=None, per=24,
                    banks=0, n_halves=None, ready=None):
                h0, n = (first, n_halves) if first is not None else SPAN[J]
                count = J // 3 if i is None else i * 2 + J // 3
                if J >= 3:
                    pe.wait_ge(evac[J % 3], count)
                nk = 1024 // wide
                for q in range(n):
                    h = h0 + q
                    if ready:
                        ready(q)
                    pe.wait_ge(lo_ready, h + 1 if i is None else i * per + h + 1)
                    w_h = hi[:, h % HALVES, :].rearrange("p (k c) -> p k c", k=nk)
                    w_l = lo[:, h % HALVES, :].rearrange("p (k c) -> p k c", k=nk)
                    todo = [(m, k) for m in range(2 if turned else (tiles or wide // P)) for k in range(nk)]
                    for m, k in todo:
                        kt = k0 + q * nk + k
                        begin = q == 0 and k == 0
                        end = q == n - 1 and k == nk - 1
                        if turned:
                            ins = three(pair2(J)[:, m, :], w_h[:, k, :], w_l[:, k, :],
                                        a_hi[:, kt, m * P:m * P + P], a_lo[:, kt, m * P:m * P + P], begin, end, False)
                        else:
                            ins = three(pair(J)[:, m, :], w_h[:, k, m * P:m * P + P], w_l[:, k, m * P:m * P + P],
                                        a_hi[:, kt, :], a_lo[:, kt, :], begin and m % 2 == 0, end, True)
                    ins.then_inc(half_used, 1)

            def column_sums(hp, i=None):
                at = hp if i is None else i + hp
                pe.wait_ge(mod_sum, 16 * (at + 1))
                if hp >= 1:
                    pe.wait_ge(modc_ready, at)
                for c in range(mod_at(hp)[1]):
                    ins = pe.matmul(ps[:, 6, c:c + 1], mod_acc(hp, i)[:, P * c:P * c + P], ones[:, 0:1],
                                    start=True, stop=True)
                ins.then_inc(colsum, 1)

            def norm_sums(s):
                if s:
                    pe.wait_ge(root_ready, s)
                both = ((wa, wb, 7), (wc, wd, 6)) if s == 2 else ((wa, wb, 7),)
                if s == 2:
                    pe.wait_ge(modc_ready, 22)
                    pe.wait_ge(S("sq2_added"), 2)
                pe.wait_ge(sq_added, 2 * s + 2)
                for first, _, b in both:
                    for k in range(4):
                        pe.matmul(ps[:, b, 0:T], ones[:], first[:, k, :], start=k == 0, stop=False)
                pe.wait_ge(sq_ready, 4 * s + 4)
                if s == 2:
                    pe.wait_ge(S("sq2_ready"), 4)
                for _, last, b in both:
                    for k in range(4):
                        ins = pe.matmul(ps[:, b, 0:T], ones[:], last[:, k, :], start=False, stop=k == 3)
                    ins.then_inc(stat_sum if b == 7 else S("sq2_sum"), 1)

            def h_there(n):
                def ready(q):
                    pe.wait_ge(h_lo_ready, 16 * n + 2 * q + 2)
                return ready

            def h_all(n):
                pe.wait_ge(h_lo_ready, 16 * n + 16)

            for a in range(2):
                pe.matmul(ps[0:16, 6 + a, 0:384], rel33[:, 16 * a:16 * a + 16], hot33[:, 384 * a:384 * a + 384],
                          start=True, stop=True).then_inc(S("bias_mm"), 1)
            pe.wait_ge(S("bias_rows_ready"), 1)
            norm_sums(0)
            for hp in range(4):
                column_sums(hp)
            job(0, h_hi, h_lo, ready=h_there(0))
            job(1, h_hi, h_lo, wide=256)
            job(2, h_hi, h_lo)
            pe.wait_ge(S("c_sq"), 1)
            pe.wait_ge(root_ready, 1)
            for k in range(2):
                ins = pe.matmul(ps[:, 7, 0:T], ones[:], csq[:, k, :], start=k == 0, stop=k == 1)
            ins.then_inc(S("c_sum"), 1)
            pe.wait_ge(evac[1], 1)
            pe.wait_ge(modc_ready, 4)
            for t in range(2):
                pe.transpose(ps[:, 6, P * t:P * t + P], va[:, P * t:P * t + P], k0_("ident", P))
            for t in range(2):
                ins = pe.transpose(ps[:, 6, 256 + 16 * t:272 + 16 * t], wiT[:, P * t:P * t + P], k0_("ident", P)[0:16, 0:16])
            ins.then_inc(S("turned"), 1)
            job(3, h_hi, h_lo)
            for b in range(3):
                pe.wait_ge(evac[b], (2, 1, 1)[b])
            for it in range(12):
                if it >= 4:
                    pe.wait_ge(S("idx_relu"), it - 3)
                for s, h in enumerate(idx_heads(it)):
                    p0 = 64 * (h % 2)
                    if it < 8:
                        o, q, n = ps[:, it % 4, T * s:T * s + T], qi[p0:p0 + 64, h // 2, P:T], T
                    else:
                        o, q, n = ps[:, it % 4, P * s:P * s + P], qi[p0:p0 + 64, h // 2, 0:P], P
                    ins = pe.matmul(o, q, g6[p0:p0 + 64, 1, 0:n], start=True, stop=True)
                ins.then_inc(S("idx_mm"), 1)
            pe.wait_ge(S("turned_out"), 1)
            column_sums(4)
            pe.wait_ge(S("idx_relu"), 12)
            job(4, h_hi, h_lo)
            job(5, h_hi, h_lo)
            column_sums(5)
            job(6, h_hi, h_lo)
            job(7, h_hi, h_lo)
            column_sums(6)
            pe.wait_ge(S("c_lo"), 2)
            job(8, c_hi, c_lo)
            job(9, c_hi, c_lo)
            job(10, c_hi, c_lo, turned=True)
            job(11, c_hi, c_lo, turned=True)
            column_sums(7)
            for b in range(3):
                pe.wait_ge(evac[b], 4)

            def attention(a):
                sr, pb = (sring, pt) if a < 2 else (sring2, pt2)
                for k in range(HEADS + 4):
                    n = 16 * a + k
                    if k < HEADS:
                        if n >= 3:
                            pe.wait_ge(att_sc, n - 2)
                        h = order(a, k)
                        if a == 2 and k % 4 == 0:
                            pe.wait_ge(S("qn_done"), k // 4 + 1)
                        for q0, c, w in ((P, 0, T), (0, T, P)):
                            o = ps[:, n % 3, c:c + w]
                            if a == 2:
                                p0 = 64 * (h % 2)
                                pe.matmul(o, qn[:, h, q0:q0 + P], kn[:, h, 0:w], start=True, stop=False)
                                ins = pe.matmul(o, qr[p0:p0 + 64, h // 2, q0:q0 + P], kr[p0:p0 + 64, 0:w],
                                                start=False, stop=True)
                            else:
                                p0 = 64 * (k % 2)
                                q = (qa, qb)[a][p0:p0 + 64, k // 2, q0:q0 + P]
                                key = g6[p0:p0 + 64, 0, 0:w] if a == 0 else kb[p0:p0 + 64, k // 2, 0:w]
                                ins = pe.matmul(o, q, key, start=True, stop=True)
                        ins.then_inc(att_scores, 1)
                    if 3 <= k < HEADS + 3:
                        m = n - 3
                        pe.wait_ge(att_prob, 2 * (m + 1))
                        if m >= 2:
                            pe.wait_ge(att_pt, m - 1)
                        for c in range(3):
                            ins = pe.transpose(ps[:, 3 + m % 2, P * c:P * c + P], sr[:, m % 4, P * c:P * c + P], k0_("ident", P))
                        ins.then_inc(att_turned, 1)
                    if k >= 4:
                        m = n - 4
                        j = k - 4
                        pe.wait_ge(att_pt, m + 1)
                        if a < 2:
                            b, p0, w = 5 + 2 * (j // 2 % 2), 64 * (j % 2), 64
                            if 16 * a + j >= 4 and j % 2 == 0:
                                pe.wait_ge(att_olo, (16 * a + j) // 2 - 1)
                            val = (lambda t: vtok[:, t, p0:p0 + 64]) if a == 0 else (lambda t: vb[:, t, 64 * j:64 * j + 64])
                        else:
                            b, p0, w = 5 + 2 * (j % 2), 0, P
                            pe.wait_ge(att_olo, 16)
                            if j >= 2:
                                pe.wait_ge(att_o, j - 1)
                            val = lambda t: vm[:, t, P * j:P * j + P]
                        o = ps[p0:p0 + w, b, :]
                        pe.matmul(o[:, P:T], val(0), pb[:, m % 2, 0:P], start=True, stop=False, skip_group_check=True)
                        pe.matmul(o[:, P:T], val(1), pb[:, m % 2, P:T], start=False, stop=False, skip_group_check=True)
                        pe.matmul(o[:, 0:P], val(0), pb[:, m % 2, T:T + P], start=False, stop=True,
                                  skip_group_check=True).then_inc(att_pv, 1)

            attention(0)
            column_sums(8)
            attention(1)
            pe.wait_ge(att_olo, 16)
            job(12, h_hi, h_lo)
            column_sums(9)
            job(13, h_hi, h_lo)
            job(14, h_hi, h_lo)
            column_sums(10)
            job(15, h_hi, h_lo)
            column_sums(11)
            norm_sums(1)
            job(J_FF, h_hi, h_lo, ready=h_there(1))
            job(J_FF + 1, h_hi, h_lo)
            with pe.Fori(0, FF_STEPS - 1) as i:
                job(J_FF + 2, h_hi, h_lo, first=112, n_halves=8, i=i)
                pe.wait_ge(S("y_lo"), i + 1)
                for c in range(4):
                    job(J_FF + 3 + c, y_hi, y_lo, first=120 + 2 * c, n_halves=2, i=i)
                column_sums(12, i)
                job(J_FF + 7, h_hi, h_lo, first=128, n_halves=8, i=i)
            pe.wait_ge(S("y_lo"), FF_STEPS)
            for c in range(4):
                job(J_V - 4 + c, y_hi, y_lo)
            norm_sums(2)
            for g in range(8):
                job(J_V + g, h_hi, h_lo, turned=True, ready=h_there(2) if g == 0 else None)
                if g % 2 == 0:
                    column_sums(22 + g // 2)
            job(J_GM, h_hi, h_lo)
            column_sums(26)
            job(J_GM + 1, h_hi, h_lo)

            def mix(s, i=None):
                pe.wait_ge(S("vs"), s * 2 + 2)
                pe.wait_ge(S("wst_masked"), s + 1)
                pe.wait_ge(modc_ready, s + 27)
                for c in range(4):
                    for t in range(2):
                        ins = pe.matmul(ps[:, 6 + c // 2, T * (c % 2) + P * t:T * (c % 2) + P * t + P],
                                        vs[:, t, P * c:P * c + P], wst[:, c // 2, :], start=True, stop=True)
                ins.then_inc(S("wmix"), 1)

            with pe.Fori(0, GM_STEPS - 1) as i:
                mix(i)
                job(J_GM + 2, h_hi, h_lo, first=2 * (U_GM + 8), n_halves=8, i=i)
                pe.wait_ge(S("y_lo"), i + FF_STEPS + 1)
                for c in range(4):
                    job(J_GM + 3 + c, y_hi, y_lo, first=2 * (U_GM + 12 + c), n_halves=2, i=i)
                pe.wait_ge(S("mixed"), i * 2 + 2)
                column_sums(27, i)
                job(J_GM + 7, h_hi, h_lo, first=2 * (U_GM + 16), n_halves=8, i=i)
            mix(GM_STEPS - 1)
            pe.wait_ge(S("y_lo"), FF_STEPS + GM_STEPS)
            for c in range(4):
                job(J_MLA - 4 + c, y_hi, y_lo)
            pe.wait_ge(S("mixed"), 2 * GM_STEPS)
            norm_sums(3)
            J = J_MLA

            def sums(e, pieces):
                pe.wait_ge(S("n_sq"), e + 1)
                if e:
                    pe.wait_ge(S("n_root"), e)
                side = (wa, wb)[e % 2]
                for o, w, t, start, stop in pieces:
                    ins = pe.matmul(o, w, side[:, t, :] if isinstance(t, int) else side[:, t[0]:t[1], :],
                                    start=start, stop=stop)
                ins.then_inc(S("n_sum"), 1)

            four = [(ps[:, 6, 0:T], ones[:], k, k == 0, k == 3) for k in range(4)]

            def wide(w):
                return [(ps[:, 6 + b, :], w, (2 * b, 2 * b + 2), True, True) for b in range(2)]

            job(J, h_hi, h_lo, ready=h_there(3))
            pe.wait_ge(evac[(J + 1) % 3], (J + 1) // 3)
            for q in range(4):
                h = SPAN[J + 1][0] + q
                pe.wait_ge(lo_ready, h + 1)
                for k in range(8):
                    ins = three(pair(J + 1)[:, q // 2, :], hi[:, h % HALVES, P * k:P * k + P], lo[:, h % HALVES, P * k:P * k + P],
                                h_hi[:, 8 * (q % 2) + k, :], h_lo[:, 8 * (q % 2) + k, :], q == 0 and k == 0, k == 7 and q % 2 == 1, True)
                ins.then_inc(half_used, 1)
                if q == 1:
                    sums(0, four)
            sums(1, [(ps[:, 6, 0:T], k0_("blk", P), 0, True, True)])
            pe.wait_ge(S("m_lo"), 4)
            for k in range(4):
                job(J + 2 + 2 * k, m_hi, m_lo)
                job(J + 3 + 2 * k, m_hi, m_lo, turned=True)
                sums(2 + k, wide(ones[:]))
            h_all(4)
            job(J + 10, h_hi, h_lo)
            job(J + 11, h_hi, h_lo)
            sums(6, four)
            for k in range(3):
                job(J + 12 + k, h_hi, h_lo)
            pe.wait_ge(S("m_lo"), 8)
            for k in range(2):
                job(J + 15 + 2 * k, m_hi, m_lo)
                job(J + 16 + 2 * k, m_hi, m_lo)
                sums(7 + k, wide(k0_("blk", P)))
            for k in range(4):
                job(J + 19 + k, m_hi, m_lo)
                if k:
                    sums(8 + k, wide(ones[:]))
            sums(12, wide(ones[:]))
            for b in range(3):
                pe.wait_ge(evac[b], len([j for j in range(J + 23) if j % 3 == b]))
            pe.wait_ge(S("kn_done"), 4)
            pe.wait_ge(S("qr_done"), 2)
            attention(2)
            pe.wait_ge(att_olo, 32)
            for k in range(4):
                job(J + 23 + k, h_hi, h_lo)

        @block.vector
        def _(dve):
            dve.memset(ones[:], 1.0).then_inc(S("ones"), 1)
            dve.memset(rel33[32:33, :], 1.0).then_inc(S("ones"), 1)
            dve.wait_ge(consts, 16 * NCONST)
            TT, STT, TS = dve.tensor_tensor, dve.scalar_tensor_tensor, dve.tensor_scalar
            MUL, ADD, SUB = ALU.mult, ALU.add, ALU.subtract

            def split(u, i=None):
                for h in range(2):
                    dve.wait_ge(hi_ready, 2 * u + h + 1 if i is None else i * 24 + 2 * u + h + 1)
                    s = (2 * u + h) % HALVES
                    TT(lo[:, s, :], raw[:, u % SLOTS, 1024 * h:1024 * h + 1024], hi[:, s, :].bitcast(F32), SUB)\
                        .then_inc(lo_ready, 1)

            def splits(a, b):
                for u in range(a, b):
                    split(u)

            def job_done(J):
                dve.wait_ge(half_used, last_half(J))

            def mod_unit(m, i=None):
                at = m if i is None else i * 8 + m
                hp = m // 8
                w = P * mod_at(hp)[1]
                acc = mod_acc(hp, i)
                slot, q = mod_slot(m)
                for j in range(2):
                    kt = 2 * (m % 8) + j
                    if j == 0:
                        dve.wait_ge(mod_full[q], 16 * mod_turn(m) if i is None else i * 64 + 16 * mod_turn(m))
                    scalar = cact[:, kt:kt + 1] if hp < MOD_A else cact[:, 16 + kt:17 + kt]
                    if kt == 0:
                        free = i + hp if i is not None else hp if hp == 22 else hp - 1
                        if i is not None or free > 0:
                            dve.wait_ge(colsum, free)
                        TS(acc[:, 0:w], slot[:, j, :], scalar, None, MUL).then_inc(mod_sum, 1)
                    else:
                        dve.wait_ge(mod_sum, 2 * at + j)
                        STT(out=acc[:, 0:w], in0=slot[:, j, :], scalar=scalar, in1=acc[:, 0:w], op0=MUL, op1=ADD)\
                            .then_inc(mod_sum, 1)

            def mod_out(hp, i=None):
                c, n = mod_at(hp)
                dve.wait_ge(colsum, hp + 1 if i is None else i + hp + 1)
                if i is None:
                    TT(modc[:, c:c + n], ps[:, 6, 0:n], c0("b_mod", c, n), ADD).then_inc(modc_ready, 1)
                else:
                    TT(modc[:, bass.ds(i * n + c, n)], ps[:, 6, 0:n], col[:, bass.ds(i * n + COLS["b_mod"] + c, n)], ADD)\
                        .then_inc(modc_ready, 1)

            def rinverse(s):
                dve.wait_ge(root_ready, s + 1)
                if s:
                    dve.wait_ge(ht_ready, (0, 16, 32, 48)[s])
                if s == 1:
                    dve.wait_ge(S("c_norm"), 2)
                dve.reciprocal(rinv[:], rs[:]).then_inc(rinv_ready, 1)
                dve.wait_ge(rinv_ready, s + 1)

            def make_h(n, scale, norm):
                if n:
                    dve.wait_ge(ht_ready, 16 * n)
                STT(out=coef[:], in0=modc[:, scale:scale + KT], scalar=1.0, in1=c0(norm, 0, KT), op0=ADD, op1=MUL)\
                    .then_inc(coef_ready, 1)
                dve.wait_ge(coef_ready, n + 1)
                if n == 2:
                    TT(coef[:], coef[:], c0("norm_final", 0, KT), MUL).then_inc(S("coef_final"), 1)
                    dve.wait_ge(S("coef_final"), 1)
                shift = scale - KT

                def rest(c):
                    for k in range(4 * c, 4 * c + 4):
                        dve.wait_ge(h_hi_ready, 16 * n + k + 1)
                        STT(out=h_lo[:, k, :], in0=(wc, wd)[c % 2][:, k % 4, :], scalar=modc[:, shift + k:shift + k + 1],
                            in1=h_hi[:, k, :].bitcast(F32), op0=ADD, op1=SUB).then_inc(h_lo_ready, 1)

                for c in range(4):
                    if c >= 2:
                        dve.wait_ge(h_lo_ready, 16 * n + 4 * (c - 1))
                    for k in range(4 * c, 4 * c + 4):
                        STT(out=(wc, wd)[c % 2][:, k % 4, :], in0=x[:, k, :], scalar=coef[:, k:k + 1], in1=rinv[:],
                            op0=MUL, op1=MUL).then_inc(ht_ready, 1)
                    if c:
                        rest(c - 1)
                rest(3)

            def mark_x(n):
                dve.memset(small[:, 32 + n:33 + n], 0.0).then_inc(x_ok, 1)

            def add_gated(J, c, gate, i=None):
                count = J // 3 if i is None else i * 2 + J // 3
                if i is not None:
                    dve.wait_ge(evac[J % 3], count - 1)
                elif J > J_MLA - 6:
                    dve.wait_ge(evac[J % 3], count)
                for m in range(4):
                    k = 4 * c + m
                    ins = STT(out=x[:, k, :], in0=pair(J)[:, m, :], scalar=modc[:, gate + k:gate + k + 1], in1=x[:, k, :],
                              op0=MUL, op1=ADD)
                ins.then_inc(evac[J % 3], 1)

            dve.wait_ge(S("cact"), 1)
            for hp in range(4):
                if hp == 3:
                    splits(0, 2)
                for m in range(8 * hp, 8 * hp + 8):
                    mod_unit(m)
                if hp:
                    mod_out(hp - 1)
            mod_out(3)
            dve.wait_ge(modc_ready, 4)
            rinverse(0)
            make_h(0, 16, "norm_attn")
            mod_unit(32)
            mod_unit(33)

            def split_mod(a, b, ahead=32):
                for u in range(a, b):
                    split(u)
                    mod_unit(ahead + u)

            split_mod(2, 10)
            dve.wait_ge(S("c_root"), 1)
            dve.wait_ge(ht_ready, 16)
            dve.reciprocal(rinv[:], rs[:]).then_inc(S("c_rinv"), 1)
            dve.wait_ge(S("c_rinv"), 1)
            for k in range(2):
                STT(out=g6[:, 2 + k, :], in0=g6[:, 2 + k, :], scalar=c0("kv_norm", k), in1=rinv[:], op0=MUL, op1=MUL)\
                    .then_inc(S("c_norm"), 1)
            for k in range(2):
                dve.wait_ge(S("c_hi"), k + 1)
                TT(c_lo[:, k, :], g6[:, 2 + k, :], c_hi[:, k, :].bitcast(F32), SUB).then_inc(S("c_lo"), 1)
            split_mod(10, 16)
            dve.wait_ge(S("turned_out"), 1)
            for it in range(12):
                dve.wait_ge(S("idx_relu"), it + 1)
                for s, h in enumerate(idx_heads(it)):
                    b, n = (1, T) if it < 8 else (0, P)
                    o = isc[:, 0:T] if it < 8 else isc[:, T:T + P]
                    r = relu[:, it % 4, n * s:n * s + n]
                    done = 2 * it + s if it < 8 else 4 * it - 16 + s
                    if h == 0:
                        TS(o, r, wtok[:, b, h:h + 1], None, MUL).then_inc(S("idx_sum"), 1)
                    else:
                        dve.wait_ge(S("idx_sum"), done)
                        STT(out=o, in0=r, scalar=wtok[:, b, h:h + 1], in1=o, op0=MUL, op1=ADD).then_inc(S("idx_sum"), 1)
            dve.wait_ge(S("idx_sum"), 32)
            TT(isc[:], isc[:], k0_("causal3", 384), ADD).then_inc(S("isc"), 1)
            dve.wait_ge(S("isc"), 1)
            split_mod(16, 17)
            for r in range(TOPK // 8):
                for b, (c, w) in enumerate(((0, T), (T, P))):
                    if r:
                        dve.wait_ge(S("top_taken"), 2 * r - 1 + b)
                    dve.max(tiny[:, 64 + 8 * b:72 + 8 * b], isc[:, c:c + w]).then_inc(S("top_max"), 1)
                for b, (c, w) in enumerate(((0, T), (T, P))):
                    dve.wait_ge(S("top_max"), 2 * r + 1 + b)
                    dve.match_replace(isc[:, c:c + w], tiny[:, 64 + 8 * b:72 + 8 * b], isc[:, c:c + w], TAKEN)\
                        .then_inc(S("top_taken"), 1)
                split_mod(17 + r, 18 + r)
                if r == 1:
                    mod_out(4)
            dve.wait_ge(S("top_taken"), 2 * (TOPK // 8))
            TS(sel[:], isc[:], TAKEN, -NEG, ALU.is_equal, MUL).then_inc(S("sel"), 1)
            dve.wait_ge(S("sel"), 1)
            TS(sel[:], sel[:], NEG, None, ADD).then_inc(S("sel"), 1)
            split_mod(25, 26)
            mod_out(5)
            split_mod(26, 32)
            mod_out(6)

            def attention(a):
                sr, tn = (sring, tiny) if a < 2 else (sring2, tiny2)
                scale = 64 ** -0.5 if a < 2 else 192 ** -0.5
                for k in range(HEADS + 6):
                    n = 16 * a + k
                    if k < HEADS:
                        q = n % 4
                        dve.wait_ge(att_scores, n + 1)
                        if a == 0:
                            dve.wait_ge(bias_full[n % 3], 32 * (n // 3 + 1))
                        if a == 1:
                            dve.wait_ge(bias_sum, k + 1)
                        if n >= 4:
                            dve.wait_ge(att_turned, n - 3)
                        STT(out=sr[:, q, :], in0=ps[:, n % 3, 0:384], scalar=scale,
                            in1=bring[:, n % 3, :] if a < 2 else k0_("causal3", 384), op0=MUL, op1=ADD).then_inc(att_sc, 1)
                        dve.wait_ge(att_sc, n + 1)
                        if n >= 4:
                            dve.wait_ge(att_negm, n - 3)
                        dve.tensor_reduce(tn[:, 16 + 2 * q:17 + 2 * q], sr[:, q, 0:T], AX, ALU.max).then_inc(att_max, 1)
                        dve.tensor_reduce(tn[:, 17 + 2 * q:18 + 2 * q], sr[:, q, T:384], AX, ALU.max).then_inc(att_max, 1)
                    if 1 <= k <= HEADS:
                        m = n - 1
                        q = m % 4
                        dve.wait_ge(att_exp, exp_count(m + 1))
                        if m >= 4:
                            dve.wait_ge(att_prob, 2 * (m - 3))
                        if a == 0:
                            TT(tn[:, 48 + 2 * q:50 + 2 * q], tn[:, 32 + 2 * q:34 + 2 * q], tn[:, 40 + 2 * q:42 + 2 * q], ADD)\
                                .then_inc(att_den, 1)
                            dve.wait_ge(att_den, m + 1)
                        src = 48 if a == 0 else 32
                        dve.reciprocal(tn[:, 56 + 2 * q:58 + 2 * q], tn[:, src + 2 * q:src + 2 + 2 * q]).then_inc(att_rden, 1)
                    if k < HEADS:
                        q = n % 4
                        dve.wait_ge(att_max, 2 * n + 2)
                        if n >= 4:
                            dve.wait_ge(att_exp, exp_count(n - 3))
                        if a == 0:
                            h = order(a, k)
                            TS(tn[:, 24 + 2 * q:26 + 2 * q], tn[:, 16 + 2 * q:18 + 2 * q], tn[:, h:h + 1], -1.0, ALU.max, MUL)\
                                .then_inc(att_negm, 1)
                        else:
                            TS(tn[:, 24 + 2 * q:26 + 2 * q], tn[:, 16 + 2 * q:18 + 2 * q], -1.0, None, MUL).then_inc(att_negm, 1)
                    if 1 <= k <= HEADS:
                        m = n - 1
                        q = m % 4
                        dve.wait_ge(att_rden, m + 1)
                        for b, (c, w) in enumerate(((0, T), (T, P))):
                            TS(sr[:, q, c:c + w], sr[:, q, c:c + w], tn[:, 56 + 2 * q + b:57 + 2 * q + b], None, MUL)\
                                .then_inc(att_prob, 1)
                    if a < 2 and k >= 6 and k % 2 == 0 and (k - 6) // 2 < 8:
                        j = (k - 6) // 2
                        dve.wait_ge(att_ohi, 8 * a + j + 1)
                        TT(h_lo[:, 8 * a + j, :], ps[:, 5 + 2 * (j % 2), 0:T], h_hi[:, 8 * a + j, :].bitcast(F32), SUB)\
                            .then_inc(att_olo, 1)
                    if a == 2:
                        if 4 <= k < HEADS + 4:
                            j = k - 4
                            dve.wait_ge(att_pv, n - 4 + 1)
                            TT(zs[:, j, :], ps[:, 5 + 2 * (j % 2), 0:T], zs[:, j, :], MUL).then_inc(att_o, 1)
                        if 5 <= k < HEADS + 5:
                            j = k - 5
                            dve.wait_ge(att_ohi, 16 + j + 1)
                            TT(h_lo[:, j, :], zs[:, j, :], h_hi[:, j, :].bitcast(F32), SUB).then_inc(att_olo, 1)
                    if a < 2 and k < HEADS and k % 2 == 1:
                        mod_unit(64 + n // 2)

            mod_out(7)
            attention(0)
            mod_out(8)
            attention(1)
            split_mod(32, 38, 48)
            job_done(12)
            add_gated(12, 0, 32)
            mark_x(0)
            split_mod(38, 42, 48)
            mod_out(9)
            job_done(13)
            add_gated(13, 1, 32)
            mark_x(1)
            split_mod(42, 46, 48)
            job_done(14)
            add_gated(14, 2, 32)
            mark_x(2)
            split_mod(46, 48, 48)
            mod_out(10)
            splits(48, 50)
            job_done(15)
            add_gated(15, 3, 32)
            mark_x(3)
            mod_out(11)
            dve.wait_ge(x_ok, 4)
            dve.wait_ge(modc_ready, 12)
            rinverse(1)
            make_h(1, 64, "norm_ffn")

            def convolve(s, i, channels):
                J = J_FF if i is None else J_FF + 2
                if i is None:
                    dve.tensor_copy(cwi[:], c0("conv", 0, 16)).then_inc(S("cwi"), 1)
                else:
                    dve.wait_ge(S("silu"), 4 * s)
                    dve.wait_ge(S("conv"), 12 * s)
                    dve.tensor_copy(cwi[:], col[:, bass.ds(s * 16 + COLS["conv"], 16)]).then_inc(S("cwi"), 1)
                dve.wait_ge(S("cwi"), s + 1)
                dve.wait_ge(evac[J % 3], channels)
                for j in range(3):
                    for m in range(4):
                        if j == 0:
                            TS(wa[:, m, :], ubuf[:, m, 2:2 + T], cwi[:, 3 * m + 2:3 * m + 3], None, MUL).then_inc(S("conv"), 1)
                        else:
                            dve.wait_ge(S("conv"), s * 12 + 4 * j - 3 + m)
                            STT(out=wa[:, m, :], in0=ubuf[:, m, 2 - j:2 - j + T], scalar=cwi[:, 3 * m + 2 - j:3 * m + 3 - j],
                                in1=wa[:, m, :], op0=MUL, op1=ADD).then_inc(S("conv"), 1)

            def gate_y(s, used):
                dve.wait_ge(half_used, used)
                dve.wait_ge(S("silu"), 4 * s + 4)
                TT(wc[:], wb[:], pair(J_FF + 1), MUL).then_inc(S("y"), 1)

            def y_rest(s, rounded, J):
                dve.wait_ge(evac[J % 3], rounded)
                TT(y_lo[:], wc[:], y_hi[:].bitcast(F32), SUB).then_inc(S("y_lo"), 1)

            def add_part(J, c, i=None):
                dve.wait_ge(evac[J % 3], J // 3 - 1 if i is None else i * 2 + J // 3 - 1)
                TT(facc[:, 4 * c:4 * c + 4, :], pair(J), facc[:, 4 * c:4 * c + 4, :], ADD).then_inc(evac[J % 3], 1)

            splits(50, 54)
            dve.memset(ubuf[:, :, 0:2], 0.0).then_inc(S("zeroed"), 1)
            dve.memset(facc[:], 0.0).then_inc(S("facc_zero"), 1)
            dve.wait_ge(S("facc_zero"), 1)
            convolve(0, None, J_FF // 3 + 1)
            splits(54, 56)
            with dve.Fori(0, FF_STEPS - 1) as i:
                for k in range(12):
                    split(56 + k, i)
                    if k < 8:
                        mod_unit(96 + k, i)
                    if k == 1:
                        gate_y(i, i * 24 + 2 * 56)
                        y_rest(i, i * 2 + (J_FF + 1) // 3 + 1, J_FF + 1)
                    if k == 5:
                        convolve(i + 1, i, i * 2 + (J_FF + 2) // 3 + 1)
                    if 6 <= k < 10:
                        dve.wait_ge(half_used, i * 24 + 2 * (61 + k - 6))
                        add_part(J_FF + 3 + k - 6, k - 6, i)
                    if k == 11:
                        mod_out(12, i)
            gate_y(FF_STEPS - 1, 2 * (U_V - 4))
            y_rest(FF_STEPS - 1, (FF_STEPS - 1) * 2 + (J_FF + 1) // 3 + 1, J_FF + 1)
            mod_v = 22 * 8 - (U_V - 4)
            split_mod(U_V - 4, U_V - 2, mod_v)
            for c in range(4):
                split_mod(U_V - 2 + c, U_V - 1 + c, mod_v)
                job_done(J_V - 4 + c)
                add_part(J_V - 4 + c, c)
                dve.wait_ge(evac[(J_V - 4 + c) % 3], (J_V - 4 + c) // 3 + 1)
                for k in range(4 * c, 4 * c + 4):
                    STT(out=x[:, k, :], in0=facc[:, k, :], scalar=modc[:, 80 + k:81 + k], in1=x[:, k, :], op0=MUL, op1=ADD)
                mark_x(4 + c)
            dve.wait_ge(stat_sum, 3)
            dve.wait_ge(rinv_ready, 2)
            TS(rs[:], ps[:, 7, 0:T], 1.0 / D, EPS, MUL, ADD).then_inc(S("ff_norm"), 1)
            dve.wait_ge(S("ff_norm"), 1)
            dve.wait_ge(ht_ready, 32)
            dve.reciprocal(rinv[:], rs[:]).then_inc(S("ff_norm"), 1)
            dve.wait_ge(S("ff_norm"), 2)
            dve.wait_ge(S("sq2_sum"), 1)
            STT(out=rinv[:], in0=ps[:, 6, 0:T], scalar=1.0 / D, in1=rinv[:], op0=MUL, op1=MUL).then_inc(S("ff_norm"), 1)
            dve.wait_ge(root_ready, 3)
            TT(rinv[:], rs[:], rinv[:], MUL).then_inc(S("ff_norm"), 1)
            dve.wait_ge(S("ff_norm"), 4)
            dve.reciprocal(rinv[:], rinv[:]).then_inc(rinv_ready, 1)
            dve.wait_ge(rinv_ready, 3)
            dve.wait_ge(x_ok, 8)
            make_h(2, 112, "norm_a")

            def finish_x():
                dve.reciprocal(rs[:], rs[:]).then_inc(S("ff_norm"), 1)
                dve.wait_ge(S("ff_norm"), 5)
                dve.wait_ge(ht_ready, 48)
                for k in range(KT):
                    STT(out=x[:, k, :], in0=x[:, k, :], scalar=c0("norm_final", k), in1=rs[:], op0=MUL, op1=MUL)
                mark_x(8)

            def moments(g):
                dve.wait_ge(evac[(J_V + g) % 3], (J_V + g) // 3 + 1)
                for t in range(2):
                    dve.bn_stats(stats[:, t, g, :], v[:, t, 512 * g:512 * g + 512]).then_inc(S("moments"), 1)

            for g in range(8):
                for k in range(4):
                    u = U_V + 4 * g + k
                    if u >= U_V + 2:
                        split_mod(u, u + 1, mod_v)
                    if g == 1 and k == 2:
                        finish_x()
                    if g and k == 1:
                        moments(g - 1)
                    if g % 2 and k == 2:
                        mod_out(22 + g // 2)
            split_mod(U_GM, U_GM + 2, mod_v)
            moments(7)
            dve.wait_ge(S("moments"), 16)
            for t in range(2):
                ins = dve.bn_aggr(mv[:, t, :], stats[:, t, :, :])
            ins.then_inc(S("v_var"), 1)
            dve.wait_ge(S("v_root"), 1)
            dve.reciprocal(rstd[:], rstd[:]).then_inc(S("rstd"), 1)
            dve.wait_ge(S("rstd"), 1)
            dve.wait_ge(S("v_var"), 1)
            for t in range(2):
                TS(v[:, t, :], v[:, t, :], mv[:, t, 0:1], rstd[:, t:t + 1], SUB, MUL).then_inc(S("v_norm"), 1)
            split_mod(U_GM + 2, U_GM + 4, mod_v)
            splits(U_GM + 4, U_GM + 6)
            mod_out(26)
            splits(U_GM + 6, U_GM + 8)

            def gm_gate(s, used):
                J = J_GM + 1
                dve.wait_ge(S("tanh"), s + 1)
                dve.wait_ge(half_used, used)
                STT(out=wb[:], in0=wb[:], scalar=1.0, in1=pair(J), op0=ADD, op1=MUL).then_inc(S("gm_a"), 1)
                dve.wait_ge(S("gm_a"), 2 * s + 1)
                TT(wb[:], wb[:], wa[:], MUL).then_inc(S("gm_a"), 1)
                dve.wait_ge(S("wmix"), s + 1)
                dve.wait_ge(S("y_lo"), s + FF_STEPS)
                for g in range(2):
                    TT(wc[:].rearrange("p (g c) t -> p g (c t)", g=2)[:, g, :].rearrange("p (a t) -> p a t", a=4),
                       ps[:, 6 + g, :].rearrange("p (a t) -> p a t", a=4),
                       bsrow[:, g:g + 1, :].to_broadcast([P, 4, P]), ADD).then_inc(S("mixed"), 1)
                dve.wait_ge(S("mixed"), s * 2 + 2)
                dve.wait_ge(S("gm_a"), 2 * s + 2)
                STT(out=wc[:], in0=wc[:], scalar=0.5, in1=wb[:], op0=MUL, op1=MUL).then_inc(S("y"), 1)

            for b in range(3):
                dve.wait_ge(evac[b], len([j for j in range(J_GM) if j % 3 == b]))
            dve.wait_ge(x_ok, 9)
            with dve.Fori(0, GM_STEPS - 1) as i:
                for k in range(12):
                    split(U_GM + 8 + k, i)
                    if k < 8:
                        mod_unit(216 + k, i)
                    if k == 1:
                        gm_gate(i, i * 24 + 2 * (U_GM + 8))
                        y_rest(i, i * 2 + (J_GM + 1) // 3 + 1, J_GM + 1)
                    if 6 <= k < 10:
                        dve.wait_ge(half_used, i * 24 + 2 * (U_GM + 13 + k - 6))
                        add_gated(J_GM + 3 + k - 6, k - 6, 128, i)
                    if k == 11:
                        mod_out(27, i)
            gm_gate(GM_STEPS - 1, 2 * (U_MLA - 4))
            y_rest(GM_STEPS - 1, (GM_STEPS - 1) * 2 + (J_GM + 1) // 3 + 1, J_GM + 1)
            splits(U_MLA - 4, U_MLA - 2)
            for c in range(4):
                splits(U_MLA - 2 + c, U_MLA - 1 + c)
                job_done(J_MLA - 4 + c)
                add_gated(J_MLA - 4 + c, c, 128)
                mark_x(9 + c)
            dve.wait_ge(x_ok, 13)
            rinverse(3)
            U, J = U_MLA, J_MLA
            make_h(3, 160, "norm_kv")
            splits(U + 2, U + 6)

            def inverse(e, n):
                side = (wc, wd)[e % 2][:].rearrange("p a t -> p (a t)")[:, 0:n]
                dve.wait_ge(S("n_root"), e + 1)
                dve.reciprocal(side, side).then_inc(S("n_rinv"), 1)
                dve.wait_ge(S("n_rinv"), e + 1)
                return (wc, wd)[e % 2]

            def latent(e, j, buf, norm):
                r = inverse(e, T)
                for k in range(4):
                    STT(out=buf[:, k, :], in0=buf[:, k, :], scalar=c0(norm, k), in1=r[:, 0, :], op0=MUL, op1=MUL)\
                        .then_inc(S("n_c"), 1)
                dve.wait_ge(S("n_c"), 4 * j + 4)
                dve.memset(small[:, 8 + e:9 + e], 0.0).then_inc(S("n_used"), 1)

            def latent_rest(j, buf):
                for k in range(4):
                    dve.wait_ge(S("m_hi"), 4 * j + k + 1)
                    TT(m_lo[:, k, :], buf[:, k, :], m_hi[:, k, :].bitcast(F32), SUB).then_inc(S("m_lo"), 1)

            latent(0, 0, kn, "g_kva")
            splits(U + 6, U + 7)
            latent_rest(0, kn)
            splits(U + 7, U + 8)
            r = inverse(1, T)
            STT(out=kr[:], in0=pair(J + 1)[:, 0, :], scalar=c0("g_kr"), in1=r[:, 0, :], op0=MUL, op1=MUL).then_inc(S("kr"), 1)
            STT(out=r[:, 1, :], in0=pair(J + 1)[:, 1, :], scalar=c0("g_krs"), in1=r[:, 0, :], op0=MUL, op1=MUL).then_inc(evac[(J + 1) % 3], 1)
            dve.wait_ge(evac[(J + 1) % 3], (J + 1) // 3 + 1)
            dve.wait_ge(S("kr"), 1)
            TT(kr[:], kr[:], k0_("cos", T), MUL).then_inc(S("kr"), 1)
            TT(r[:, 1, :], r[:, 1, :], k0_("sin", T), MUL).then_inc(S("kr"), 1)
            dve.wait_ge(S("kr"), 3)
            TT(kr[:], kr[:], r[:, 1, :], ADD).then_inc(S("n_used"), 1)
            dve.wait_ge(S("n_used"), 2)
            make_h(4, 192, "norm_b")

            def used(e):
                dve.memset(small[:, 8 + e:9 + e], 0.0).then_inc(S("n_used"), 1)

            def normed(e, J, part, done):
                r = inverse(e, 1024)
                dve.wait_ge(evac[J % 3], J // 3 + 1)
                TT(part, part, r[:], MUL).then_inc(S(done), 1)
                used(e)

            for k in range(4):
                splits(U + 8 + 2 * k, U + 10 + 2 * k)
                normed(2 + k, J + 2 + 2 * k, kn[:, 4 * k:4 * k + 4, :], "kn_done")
            splits(U + 16, U + 24)
            latent(6, 1, qr, "g_qa")
            latent_rest(1, qr)
            splits(U + 24, U + 37)
            for k in range(2):
                splits(U + 37 + 2 * k, U + 38 + 2 * k)
                q4 = qr[:, 4 * k:4 * k + 4, :]
                dve.wait_ge(S("qr_turned"), 2 * k + 2)
                TT(q4, q4, qrs[:], ADD).then_inc(S("qr_sum"), 1)
                r = inverse(7 + k, 1024)
                dve.wait_ge(S("qr_sum"), k + 1)
                TT(q4, q4, r[:], MUL).then_inc(S("qr_done"), 1)
                used(7 + k)
                splits(U + 38 + 2 * k, U + 39 + 2 * k)
            for k in range(4):
                if k < 3:
                    splits(U + 41 + k, U + 42 + k)
                inverse(9 + k, 1024)
            attention(2)
            splits(U + 44, U + 46)
            for k in range(4):
                splits(U + 46 + 4 * k, min(U + 50 + 4 * k, UNITS))
                job_done(J + 23 + k)
                add_gated(J + 23 + k, k, 208)
            mark_x(13)

        @block.gpsimd
        def _(pool):
            def add_squares(s):
                for c in range(1, 3):
                    pool.wait_ge(sq_ready, 4 * s + c + 1)
                    if c == 2:
                        pool.wait_ge(sq_added, 2 * s + 1)
                    pool.tensor_tensor(wa[:], wa[:], wb[:], ALU.add).then_inc(sq_added, 1)
                    if s == 2:
                        pool.wait_ge(S("sq2_ready"), c + 1)
                        if c == 2:
                            pool.wait_ge(S("sq2_added"), 1)
                        pool.tensor_tensor(wc[:], wc[:], wd[:], ALU.add).then_inc(S("sq2_added"), 1)

            add_squares(0)
            pool.wait_ge(S("sel"), 2)
            for n in range(16, 32):
                pool.wait_ge(bias_full[n % 3], 32 * (n // 3 + 1))
                pool.tensor_tensor(bring[:, n % 3, :], bring[:, n % 3, :], sel[:], ALU.add).then_inc(bias_sum, 1)

            def values(s, first=False):
                pool.wait_ge(S("lnrow"), s * 16 + 16)
                if not first:
                    pool.wait_ge(S("wmix"), s)
                for t in range(2):
                    pool.tensor_tensor(vs[:, t, :], v[:, t, bass.ds(s * 512, 512)], lnrow[:, 0, :], ALU.mult).then_inc(S("vs_g"), 1)
                pool.wait_ge(S("wst"), s * 16 + 16)
                for g in range(2):
                    ins = pool.tensor_tensor(wst[:, g, :], wst[:, g, :], k0_("triu", P), ALU.mult)
                ins.then_inc(S("wst_masked"), 1)
                pool.wait_ge(S("vs_g"), s * 2 + 2)
                for t in range(2):
                    pool.tensor_tensor(vs[:, t, :], vs[:, t, :], lnrow[:, 1, :], ALU.add).then_inc(S("vs"), 1)

            add_squares(1)
            add_squares(2)
            pool.wait_ge(S("v_norm"), 2)
            values(0, first=True)
            with pool.Fori(1, GM_STEPS) as i:
                values(i)
            add_squares(3)
            for k in range(2):
                J = J_MLA + 15 + 2 * k
                for n, part, by in ((J, qr[:, 4 * k:4 * k + 4, :], "cos"), (J + 1, qrs[:], "sin")):
                    pool.wait_ge(evac[n % 3], n // 3 + 1)
                    pool.tensor_tensor(part, part, k0_(by, T).unsqueeze(1).to_broadcast([P, 4, T]), ALU.mult)\
                        .then_inc(S("qr_turned"), 1)
            for k in range(4):
                J = J_MLA + 19 + k
                part = qn[:, 4 * k:4 * k + 4, :]
                pool.wait_ge(evac[J % 3], J // 3 + 1)
                pool.wait_ge(S("n_rinv"), 10 + k)
                pool.tensor_tensor(part, part, (wc, wd)[(9 + k) % 2][:], ALU.mult).then_inc(S("qn_done"), 1)


def _tiles(w):
    return w.reshape(w.shape[0] // P, P, w.shape[1])


def _units(w, width):
    k = 2048 // width
    t = w.reshape(w.shape[0] // (k * P), k, P, width).transpose(0, 2, 1, 3)
    return t.reshape(-1, P, 2048)


def _columns(vec):
    return vec.reshape(-1, P).T


def _shape_constants():
    import math
    con = np.zeros((P, NCST), np.float32)
    i, j = np.arange(P)[:, None], np.arange(P)[None, :]
    con[:, CST["ident"]:][:, :P] = i == j
    causal = np.where(j <= i, 0, NEG)
    con[:, CST["causal3"]:][:, P:384] = np.concatenate([causal, causal], 1)
    con[:, CST["triu"]:][:, :P] = i <= j
    con[:, CST["blk"]:][:, :P] = i // 64 == j // 64
    pos = np.arange(T, dtype=np.float32)
    freq = np.float32(10000.0) ** (-np.arange(0, 64, 2, dtype=np.float32) / np.float32(64))
    ang = (pos[:, None] * freq[None, :]).astype(np.float32).T
    con[:, CST["cos"]:][:, :T] = np.concatenate([np.cos(ang)] * 4, 0)
    con[:, CST["sin"]:][:, :T] = np.concatenate([-np.sin(ang), np.sin(ang)] * 2, 0)
    dist = 255 - np.arange(384)
    n = np.maximum(dist, 0)
    nf = np.maximum(n, 1).astype(np.float32)
    large = 16 + (np.log(nf / np.float32(16)) / np.float32(math.log(128 / 16)) * np.float32(16)).astype(np.int32)
    bucket = np.where(n < 16, n, np.minimum(large, 31))
    hot = np.zeros((33, 2, 384), np.float32)
    window = [(dist >= 0) & (dist < 128), dist >= 0]
    for a in range(2):
        hot[bucket[window[a]], a, np.nonzero(window[a])[0]] = 1
        hot[32, a] = np.where(window[a], 0, NEG)
    return con, hot.reshape(33, 768)


def kernel(x, c, w_mod, b_mod, norm_attn, w_in, attn_sinks, kv_norm, w_uk, w_uv, rel_bias, w_out,
           norm_ffn, w_up, conv_w, conv_b, w_down, norm_final, c_2, ada_w_2, ada_b_2, norm_g_2,
           a_w_in_2, a_ln_g_2, a_ln_b_2, a_w_s_2, a_b_s_2, a_w_out_2, kv_ada_w_2, kv_ada_b_2,
           kv_norm_g_2, kv_w_dkv_2, kv_g_kva_2, kv_w_ukv_2, kv_g_kn_2, kv_g_kr_2, b_w_in_2, b_g_qa_2,
           b_w_uq_2, b_g_qn_2, b_g_qr_2, b_w_out_2):
    import concourse.bacc as bacc
    from concourse.bass_utils import run_bass_kernel_spmd

    (x, c, w_mod, b_mod, norm_attn, w_in, attn_sinks, kv_norm, w_uk, w_uv, rel_bias, w_out,
     norm_ffn, w_up, conv_w, conv_b, w_down, norm_final, c_2, ada_w_2, ada_b_2, norm_g_2,
     a_w_in_2, a_ln_g_2, a_ln_b_2, a_w_s_2, a_b_s_2, a_w_out_2, kv_ada_w_2, kv_ada_b_2,
     kv_norm_g_2, kv_w_dkv_2, kv_g_kva_2, kv_w_ukv_2, kv_g_kn_2, kv_g_kr_2, b_w_in_2, b_g_qa_2,
     b_w_uq_2, b_g_qn_2, b_g_qr_2, b_w_out_2) = [np.asarray(a) for a in (
         x, c, w_mod, b_mod, norm_attn, w_in, attn_sinks, kv_norm, w_uk, w_uv, rel_bias, w_out,
         norm_ffn, w_up, conv_w, conv_b, w_down, norm_final, c_2, ada_w_2, ada_b_2, norm_g_2,
         a_w_in_2, a_ln_g_2, a_ln_b_2, a_w_s_2, a_b_s_2, a_w_out_2, kv_ada_w_2, kv_ada_b_2,
         kv_norm_g_2, kv_w_dkv_2, kv_g_kva_2, kv_w_ukv_2, kv_g_kn_2, kv_g_kr_2, b_w_in_2, b_g_qa_2,
         b_w_uq_2, b_g_qn_2, b_g_qr_2, b_w_out_2)]

    w = w_in[0]
    qa, ka, va, qb, ckv, qi, ki, wi = np.split(w, [1024, 1152, 1280, 2304, 2560, 3584, 3648], axis=1)
    qa = qa.reshape(D, 2, 8, 64).transpose(0, 2, 1, 3).reshape(D, 1024)
    parts = [_units(np.concatenate([ka, ki, ki, ckv], 1), 512),
             _units(np.concatenate([va, wi, np.zeros((D, 112), w.dtype)], 1), 256)]
    parts += [_units(m[:, 512 * g:512 * g + 512], 512) for m in (qi, qa, qb) for g in range(2)]
    for m in (w_uk[0], w_uv[0]):
        m = m.transpose(1, 0, 2).reshape(256, 1024)
        parts.append(np.concatenate([m[:, :512].reshape(2, P, 512).transpose(1, 0, 2).reshape(P, 1024),
                                     m[:, 512:].reshape(2, P, 512).transpose(1, 0, 2).reshape(P, 1024)], 1)[None])
    m = np.concatenate([w_out[0][:1024].reshape(2, 8, 64, D).transpose(1, 0, 2, 3).reshape(1024, D), w_out[0][1024:]], 0)
    parts += [_units(m[:, 512 * g:512 * g + 512], 512) for g in range(4)]

    def up(m, s):
        return _units(m[:, 512 * s:512 * s + 512], 512)

    def down(m, s):
        return [_units(m[512 * s:512 * s + 512, 512 * g:512 * g + 512], 512) for g in range(4)]

    def mlp(a, b, m, steps):
        got = [up(a, 0), up(b, 0)]
        for s in range(1, steps):
            got += [up(a, s)] + down(m, s - 1) + [up(b, s)]
        return got + down(m, steps - 1)

    parts += mlp(w_up[0][:, :D_FF], w_up[0][:, D_FF:], w_down[0], FF_STEPS)
    u, v, z = (a_w_in_2[0][:, GM * n:GM * n + GM] for n in range(3))
    parts += [up(v, s) for s in range(GM_STEPS)] + mlp(u, z, a_w_out_2[0], GM_STEPS)
    w = kv_w_dkv_2
    parts.append(_units(w[:, :512], 512))
    r, rs = w[:, 512:], np.concatenate([w[:, 544:], w[:, 512:544]], 1)
    parts += [_units(np.concatenate([m, m], 1), P) for m in (r, rs)]
    w = kv_w_ukv_2.reshape(512, 16, 256)
    parts += [up(m, s) for s in range(4) for m in (w[:, :, :P].reshape(512, 2048), w[:, :, P:].reshape(512, 2048))]
    parts += [up(b_w_in_2[0], s) for s in range(5)]
    w = b_w_uq_2[0].reshape(512, 16, 192)
    r = w[:, :, P:]
    for s in range(2):
        parts += [up(m.reshape(512, 1024), s) for m in (r, np.concatenate([r[:, :, 32:], r[:, :, :32]], 2))]
    parts += [up(w[:, :, :P].reshape(512, 2048), s) for s in range(4)]
    parts += [up(b_w_out_2[0], s) for s in range(4)]
    stream = np.concatenate(parts, 0)
    assert stream.shape == (UNITS, P, 2048)

    mods_a = np.concatenate([_units(w_mod[0][:, 1024 * n:1024 * n + 1024], 1024) for n in range(MOD_A)], 0)
    m = np.concatenate([ada_w_2[0], kv_ada_w_2, ada_w_2[1], np.zeros((D, P * MOD_COLS - 14 * D), w.dtype)], 1)
    mods_b = np.concatenate([m[:, 768 * n:768 * n + 768].reshape(8, 2, P, 768).transpose(0, 2, 1, 3).reshape(8, P, 1536)
                             for n in range(MOD_B)], 0)

    conv = np.concatenate([conv_w[0].T, conv_b[0][:, None]], 1)
    conv = conv.reshape(FF_STEPS, 4, P, 4)
    conv = np.concatenate([conv[..., :3].transpose(2, 0, 1, 3).reshape(P, FF_STEPS, 12),
                           conv[..., 3].transpose(2, 0, 1).reshape(P, FF_STEPS, 4)], 2).reshape(P, -1)
    b_all = np.concatenate([b_mod[0], ada_b_2[0], kv_ada_b_2, ada_b_2[1], np.zeros(P * MOD_COLS - 14 * D, b_mod.dtype)])

    def twice(g):
        return np.concatenate([g, g])

    def swapped(g):
        return np.concatenate([g[32:], g[:32]])

    cols = np.concatenate([_columns(m) for m in (b_all, norm_attn[0], norm_ffn[0], norm_final, norm_g_2[0], kv_norm_g_2,
                                                 norm_g_2[1])] + [conv] +
                          [_columns(m) for m in (kv_norm[0], kv_g_kva_2, b_g_qa_2[0], kv_g_kn_2, b_g_qn_2[0],
                                                 twice(kv_g_kr_2), twice(swapped(kv_g_kr_2)), twice(b_g_qr_2[0]),
                                                 twice(swapped(b_g_qr_2[0])), c[0], c_2[0])], 1)
    con, hot = _shape_constants()
    rowpar = np.concatenate([a_ln_g_2[0].reshape(8, 512), a_ln_b_2[0].reshape(8, 512), a_b_s_2[0].reshape(8, 256)], 1)
    wsT = a_w_s_2[0].transpose(0, 2, 1).reshape(8, 2, P, P).transpose(0, 2, 1, 3).reshape(8, P, 256)
    arrays = {"stream": stream, "mods_a": mods_a, "mods_b": mods_b, "xT": x[0].T.reshape(KT, P, T).transpose(1, 0, 2), "cols": cols, "cst": con,
              "relb": rel_bias, "onehot": hot, "sinks": attn_sinks[0], "rowpar": rowpar, "wsT": wsT}
    arrays = {n: np.ascontiguousarray(a) for n, a in arrays.items()}

    nc = bacc.Bacc("TRN2", target_bir_lowering=False, num_devices=1)
    args = [nc.dram_tensor(n, a.shape, F32, kind="ExternalInput").ap() for n, a in arrays.items()]
    out = nc.dram_tensor("out", (P, KT, T), F32, kind="ExternalOutput").ap()
    build(nc, *args, out)
    got = run_bass_kernel_spmd(nc, [arrays], core_ids=[0]).results[0]["out"]
    return np.ascontiguousarray(np.asarray(got).transpose(2, 1, 0).reshape(1, T, D))
```
